# Optimizing a Trainium2 kernel written in Bass

```python
import jax, jax.numpy as jnp
from jax import lax
import numpy as np
import math

D_MODEL = 1024
BATCH = 1
SEQ = 256
DEPTH = 1

ROPE_THETA = 500000.0
EPS = 1e-6
Q_BLOCK = 128
A_HEADS = 8
A_KV_HEADS = 2
A_HEAD_DIM = 64
A_ROT_DIM = A_HEAD_DIM // 4
IDX_HEADS = 8
IDX_DIM = 64
IDX_ROT_DIM = IDX_DIM // 4
INDEX_TOPK_MAX = 256
B_HEADS = 8
B_Q_RANK = 256
B_KV_RANK = 128
B_NOPE_DIM = 64
B_ROPE_DIM = 32
B_V_DIM = 64
D_FF = 2816
CONV_WIDTH = 3

A_Q_W = A_HEADS * A_HEAD_DIM
A_KV_W = A_KV_HEADS * A_HEAD_DIM
IDX_Q_W = IDX_HEADS * IDX_DIM
B_OUT_W = B_HEADS * B_V_DIM
IN_SPLITS = [A_Q_W, A_KV_W, A_KV_W, IDX_Q_W, IDX_DIM, IDX_HEADS,
             B_Q_RANK, B_KV_RANK, B_ROPE_DIM, D_MODEL, D_MODEL]
IN_PROJ_W = int(sum(IN_SPLITS))
IN_OFFSETS = [int(o) for o in np.cumsum(IN_SPLITS)[:-1]]


def rmsnorm(x, g):
    xf = x.astype(jnp.float32)
    y = xf * lax.rsqrt(jnp.mean(xf * xf, axis=-1, keepdims=True) + EPS)
    return (y * g.astype(jnp.float32)).astype(x.dtype)

def rope_tables(positions, rot_dim):
    inv = ROPE_THETA ** (-jnp.arange(0, rot_dim, 2, dtype=jnp.float32) / rot_dim)
    ang = positions.astype(jnp.float32)[..., None] * inv
    return jnp.cos(ang), jnp.sin(ang)

def apply_rope(x, cos, sin, rot_dim):
    xr = x[..., :rot_dim].astype(jnp.float32)
    x1, x2 = jnp.split(xr, 2, axis=-1)
    c = cos[:, :, None, :]
    s = sin[:, :, None, :]
    rot = jnp.concatenate([x1 * c - x2 * s, x1 * s + x2 * c], axis=-1).astype(x.dtype)
    return jnp.concatenate([rot, x[..., rot_dim:]], axis=-1)

def to_blocks(t, nb):
    b = t.shape[0]
    return jnp.moveaxis(t.reshape(b, nb, Q_BLOCK, *t.shape[2:]), 1, 0)

def indexed_sparse_attention(q, k, v, qi, ki, wi, pos, topk):
    b, s = pos.shape
    nb = s // Q_BLOCK
    group = A_HEADS // A_KV_HEADS
    scale = A_HEAD_DIM ** -0.5
    bidx = jnp.arange(b)[:, None, None]

    def one_block(args):
        qb, qib, wib, posb = args
        dots = jnp.einsum('bqhd,bsd->bqhs', qib, ki, preferred_element_type=jnp.float32)
        iscore = jnp.einsum('bqh,bqhs->bqs', wib.astype(jnp.float32), jax.nn.relu(dots))
        causal = pos[:, None, :] <= posb[:, :, None]
        iscore = jnp.where(causal, iscore, -jnp.inf)
        _, idx = lax.top_k(iscore, topk)
        ksel = k[bidx, idx]
        vsel = v[bidx, idx]
        valid = pos[bidx, idx] <= posb[:, :, None]
        qg = qb.reshape(b, Q_BLOCK, A_KV_HEADS, group, A_HEAD_DIM)
        sc = jnp.einsum('bqgrd,bqkgd->bqgrk', qg, ksel, preferred_element_type=jnp.float32) * scale
        sc = jnp.where(valid[:, :, None, None, :], sc, -jnp.inf)
        p = jax.nn.softmax(sc, axis=-1)
        o = jnp.einsum('bqgrk,bqkgd->bqgrd', p.astype(v.dtype), vsel)
        return o.reshape(b, Q_BLOCK, A_HEADS * A_HEAD_DIM)

    out = lax.map(one_block, (to_blocks(q, nb), to_blocks(qi, nb), to_blocks(wi, nb), to_blocks(pos, nb)))
    return jnp.moveaxis(out, 0, 1).reshape(b, s, A_HEADS * A_HEAD_DIM)

def latent_attention(q_nope, q_rope, k_nope, k_rope, v, pos):
    b, s = pos.shape
    nb = s // Q_BLOCK
    scale = (B_NOPE_DIM + B_ROPE_DIM) ** -0.5

    def one_block(args):
        qn, qr, posb = args
        sc = (jnp.einsum('bqhd,bshd->bhqs', qn, k_nope, preferred_element_type=jnp.float32)
              + jnp.einsum('bqhd,bsd->bhqs', qr, k_rope, preferred_element_type=jnp.float32)) * scale
        causal = pos[:, None, None, :] <= posb[:, None, :, None]
        sc = jnp.where(causal, sc, -jnp.inf)
        p = jax.nn.softmax(sc, axis=-1)
        o = jnp.einsum('bhqs,bshd->bqhd', p.astype(v.dtype), v)
        return o.reshape(b, Q_BLOCK, B_HEADS * B_V_DIM)

    out = lax.map(one_block, (to_blocks(q_nope, nb), to_blocks(q_rope, nb), to_blocks(pos, nb)))
    return jnp.moveaxis(out, 0, 1).reshape(b, s, B_HEADS * B_V_DIM)

def causal_depthwise_conv(u, w, bias):
    s = u.shape[1]
    up = jnp.pad(u, ((0, 0), (CONV_WIDTH - 1, 0), (0, 0)))
    y = bias
    for j in range(CONV_WIDTH):
        y = y + w[j] * up[:, j:j + s]
    return y

def first_inputs(seed: int = 0) -> dict:
    key = jax.random.key(seed)
    ks = jax.random.split(key, 20)
    f32 = jnp.float32
    L = DEPTH

    def nrm(k, shape, fan_in):
        return jax.random.normal(k, shape, f32) * (fan_in ** -0.5)

    def gain(k, shape):
        return 1.0 + 0.02 * jax.random.normal(k, shape, f32)

    return {
        "x": jax.random.normal(ks[0], (BATCH, SEQ, D_MODEL), f32),
        "positions": jnp.broadcast_to(jnp.arange(SEQ, dtype=jnp.int32), (BATCH, SEQ)),
        "norm_mix_g": gain(ks[1], (L, D_MODEL)),
        "w_in": nrm(ks[2], (L, D_MODEL, IN_PROJ_W), D_MODEL),
        "idx_k_norm_g": gain(ks[3], (L, IDX_DIM)),
        "q_a_norm_g": gain(ks[4], (L, B_Q_RANK)),
        "kv_a_norm_g": gain(ks[5], (L, B_KV_RANK)),
        "w_uq": nrm(ks[6], (L, B_Q_RANK, B_HEADS, B_NOPE_DIM + B_ROPE_DIM), B_Q_RANK),
        "w_uk": nrm(ks[7], (L, B_KV_RANK, B_HEADS, B_NOPE_DIM), B_KV_RANK),
        "w_uv": nrm(ks[8], (L, B_KV_RANK, B_HEADS, B_V_DIM), B_KV_RANK),
        "w_branch_a": nrm(ks[9], (L, A_Q_W, D_MODEL), A_Q_W),
        "w_branch_b": nrm(ks[10], (L, B_OUT_W, D_MODEL), B_OUT_W),
        "w_out": nrm(ks[11], (L, D_MODEL, D_MODEL), D_MODEL),
        "norm_ffn_g": gain(ks[12], (L, D_MODEL)),
        "w_up": nrm(ks[13], (L, D_MODEL, 2 * D_FF), D_MODEL),
        "conv_w": nrm(ks[14], (L, CONV_WIDTH, 2 * D_FF), CONV_WIDTH),
        "conv_b": 0.01 * jax.random.normal(ks[15], (L, 2 * D_FF), f32),
        "w_down": nrm(ks[16], (L, D_FF, D_MODEL), D_FF),
        "norm_final_g": gain(ks[17], (D_MODEL,)),
    }

def first_block(x, positions, norm_mix_g, w_in, idx_k_norm_g, q_a_norm_g, kv_a_norm_g,
              w_uq, w_uk, w_uv, w_branch_a, w_branch_b, w_out, norm_ffn_g,
              w_up, conv_w, conv_b, w_down, norm_final_g):
    b, s, _ = x.shape
    topk = min(INDEX_TOPK_MAX, s // 4)
    cos_a, sin_a = rope_tables(positions, A_ROT_DIM)
    cos_i, sin_i = rope_tables(positions, IDX_ROT_DIM)
    cos_b, sin_b = rope_tables(positions, B_ROPE_DIM)
    h = x
    for l in range(DEPTH):
        hn = rmsnorm(h, norm_mix_g[l])
        proj = jnp.einsum('bsd,de->bse', hn, w_in[l])
        (a_q, a_k, a_v, i_q, i_k, i_w, b_cq, b_ckv, b_kr, g_a, g_b) = jnp.split(proj, IN_OFFSETS, axis=-1)

        a_q = apply_rope(a_q.reshape(b, s, A_HEADS, A_HEAD_DIM), cos_a, sin_a, A_ROT_DIM)
        a_k = apply_rope(a_k.reshape(b, s, A_KV_HEADS, A_HEAD_DIM), cos_a, sin_a, A_ROT_DIM)
        a_v = a_v.reshape(b, s, A_KV_HEADS, A_HEAD_DIM)
        i_q = apply_rope(i_q.reshape(b, s, IDX_HEADS, IDX_DIM), cos_i, sin_i, IDX_ROT_DIM) * (IDX_DIM ** -0.5)
        i_k = apply_rope(rmsnorm(i_k, idx_k_norm_g[l])[:, :, None, :], cos_i, sin_i, IDX_ROT_DIM)[:, :, 0, :]
        i_w = i_w * (IDX_HEADS ** -0.5)
        o_a = indexed_sparse_attention(a_q, a_k, a_v, i_q, i_k, i_w, positions, topk)

        c_q = rmsnorm(b_cq, q_a_norm_g[l])
        q_b = jnp.einsum('bsr,rhd->bshd', c_q, w_uq[l])
        q_nope = q_b[..., :B_NOPE_DIM]
        q_rope = apply_rope(q_b[..., B_NOPE_DIM:], cos_b, sin_b, B_ROPE_DIM)
        c_kv = rmsnorm(b_ckv, kv_a_norm_g[l])
        k_nope = jnp.einsum('bsr,rhd->bshd', c_kv, w_uk[l])
        v_b = jnp.einsum('bsr,rhd->bshd', c_kv, w_uv[l])
        k_rope = apply_rope(b_kr[:, :, None, :], cos_b, sin_b, B_ROPE_DIM)[:, :, 0, :]
        o_b = latent_attention(q_nope, q_rope, k_nope, k_rope, v_b, positions)

        y_a = jnp.einsum('bsc,cd->bsd', o_a, w_branch_a[l])
        y_b = jnp.einsum('bsc,cd->bsd', o_b, w_branch_b[l])
        merged = jax.nn.sigmoid(g_a) * y_a + jax.nn.sigmoid(g_b) * y_b
        h = h + jnp.einsum('bsd,de->bse', merged, w_out[l])

        hn = rmsnorm(h, norm_ffn_g[l])
        u = jnp.einsum('bsd,df->bsf', hn, w_up[l])
        u = causal_depthwise_conv(u, conv_w[l], conv_b[l])
        gate, val = jnp.split(u, 2, axis=-1)
        h = h + jnp.einsum('bsf,fd->bsd', jax.nn.silu(gate) * val, w_down[l])
    return rmsnorm(h, norm_final_g)


DEPTH_2 = 2

N_MIXERS = 2
N_A_LAYERS = (DEPTH_2 + 1) // 2
N_B_LAYERS = DEPTH_2 // 2

HGRN_EXPAND = 128
HGRN_HEADS = D_MODEL // HGRN_EXPAND
HGRN_FDIM = HGRN_HEADS * HGRN_EXPAND
HGRN_IDIM = D_MODEL // HGRN_HEADS
HGRN_CHUNK = 64

ATTN_HEADS = 8
ATTN_HEAD_DIM = D_MODEL // ATTN_HEADS
MOBA_BLOCK = 256
MOBA_TOPK = 3
MOBA_QCHUNK = 32

REL_BUCKETS = 32
REL_MAX_DISTANCE = 1024

D_FF_2 = -(-(8 * D_MODEL) // (3 * 256)) * 256
RMS_EPS = 1e-6


def rms_norm(x, g):
    xf = x.astype(jnp.float32)
    y = xf * lax.rsqrt(jnp.mean(xf * xf, axis=-1, keepdims=True) + RMS_EPS)
    return (y * g.astype(jnp.float32)).astype(x.dtype)

def t5_bucket(dist):
    n = jnp.maximum(dist, 0)
    max_exact = REL_BUCKETS // 2
    nf = jnp.maximum(n, max_exact).astype(jnp.float32)
    large = max_exact + (jnp.log(nf / max_exact) / math.log(REL_MAX_DISTANCE / max_exact)
                         * (REL_BUCKETS - max_exact)).astype(jnp.int32)
    large = jnp.minimum(large, REL_BUCKETS - 1)
    return jnp.where(n < max_exact, n, large)

def hgrn2_mixer(h, w_in, w_out, lb, out_norm):
    b_, s_, _ = h.shape
    f32 = jnp.float32
    proj = h @ w_in
    q, fz, inp, og = jnp.split(proj, [HGRN_FDIM, 2 * HGRN_FDIM, 2 * HGRN_FDIM + D_MODEL], axis=-1)
    q = jax.nn.silu(q.astype(f32))
    lbf = lb.astype(f32)
    f = lbf + (1.0 - lbf) * jax.nn.sigmoid(fz.astype(f32))
    k = 1.0 - f
    logf = jnp.log(f)
    nc = s_ // HGRN_CHUNK

    def to_chunks(t, d):
        return t.reshape(b_, nc, HGRN_CHUNK, HGRN_HEADS, d).transpose(1, 0, 3, 2, 4)

    qc = to_chunks(q, HGRN_EXPAND)
    kc = to_chunks(k, HGRN_EXPAND)
    gc = to_chunks(logf, HGRN_EXPAND)
    ic = to_chunks(inp.astype(f32), HGRN_IDIM)
    causal = jnp.tril(jnp.ones((HGRN_CHUNK, HGRN_CHUNK), dtype=bool))

    def step(state, xs):
        qb, kb, gb, ib = xs
        cum = jnp.cumsum(gb, axis=2)
        diff = cum[:, :, :, None, :] - cum[:, :, None, :, :]
        decay = jnp.exp(jnp.where(causal[:, :, None], diff, -jnp.inf))
        scores = jnp.einsum('bhtn,bhsn,bhtsn->bhts', qb, kb, decay)
        o = (jnp.einsum('bhts,bhsd->bhtd', scores, ib)
             + jnp.einsum('bhtn,bhnd->bhtd', qb * jnp.exp(cum), state))
        last = cum[:, :, -1:, :]
        state = (state * jnp.exp(last[:, :, 0, :, None])
                 + jnp.einsum('bhsn,bhsd->bhnd', kb * jnp.exp(last - cum), ib))
        return state, o

    s0 = jnp.zeros((b_, HGRN_HEADS, HGRN_EXPAND, HGRN_IDIM), f32)
    _, o = lax.scan(step, s0, (qc, kc, gc, ic))
    o = o.transpose(1, 0, 3, 2, 4).reshape(b_, s_, D_MODEL)
    o = rms_norm(o, out_norm) * jax.nn.sigmoid(og.astype(f32))
    return (o.astype(h.dtype) @ w_out).astype(h.dtype)

def moba_mixer(h, w_in, w_out, rel_table):
    b_, s_, _ = h.shape
    f32 = jnp.float32
    nh, dh = ATTN_HEADS, ATTN_HEAD_DIM
    q, k, v = jnp.split(h @ w_in, 3, axis=-1)
    heads = lambda t: t.reshape(b_, s_, nh, dh).transpose(0, 2, 1, 3)
    q, k, v = heads(q), heads(k), heads(v)
    nb = -(-s_ // MOBA_BLOCK)
    pad = nb * MOBA_BLOCK - s_
    kp = jnp.pad(k, ((0, 0), (0, 0), (0, pad), (0, 0)))
    vp = jnp.pad(v, ((0, 0), (0, 0), (0, pad), (0, 0)))
    kb = kp.reshape(b_, nh, nb, MOBA_BLOCK, dh)
    vb = vp.reshape(b_, nh, nb, MOBA_BLOCK, dh)
    kmean = jnp.mean(kb.astype(f32), axis=3)
    scale = dh ** -0.5
    nqc = s_ // MOBA_QCHUNK
    qch = q.reshape(b_, nh, nqc, MOBA_QCHUNK, dh).transpose(2, 0, 1, 3, 4)
    bi = jnp.arange(b_)[:, None, None, None]
    hi = jnp.arange(nh)[None, :, None, None]
    table_t = rel_table.T
    topk = min(MOBA_TOPK, nb)
    kk = topk * MOBA_BLOCK

    def chunk(args):
        c, qb = args
        q0 = c * MOBA_QCHUNK
        qpos = q0 + jnp.arange(MOBA_QCHUNK)
        j = q0 // MOBA_BLOCK
        gate = jnp.einsum('bhqd,bhnd->bhqn', qb.astype(f32), kmean)
        gate = jnp.where(jnp.arange(nb) < j, gate, -jnp.inf)
        _, sel = lax.top_k(gate, topk)
        sel_ok = jnp.arange(topk) < j
        ks = kb[bi, hi, sel]
        vs = vb[bi, hi, sel]
        s_sel = jnp.einsum('bhqd,bhqkpd->bhqkp', qb, ks).astype(f32) * scale
        kpos_sel = sel[..., None] * MOBA_BLOCK + jnp.arange(MOBA_BLOCK)
        bias_sel = table_t[hi[..., None], t5_bucket(qpos[:, None, None] - kpos_sel)]
        s_sel = jnp.where(sel_ok[:, None], s_sel + bias_sel.astype(f32), -jnp.inf)
        kown = lax.dynamic_slice_in_dim(kp, j * MOBA_BLOCK, MOBA_BLOCK, axis=2)
        vown = lax.dynamic_slice_in_dim(vp, j * MOBA_BLOCK, MOBA_BLOCK, axis=2)
        dist_own = qpos[:, None] - (j * MOBA_BLOCK + jnp.arange(MOBA_BLOCK))[None, :]
        bias_own = rel_table[t5_bucket(dist_own)].transpose(2, 0, 1).astype(f32)
        s_own = jnp.einsum('bhqd,bhpd->bhqp', qb, kown).astype(f32) * scale + bias_own
        s_own = jnp.where(dist_own >= 0, s_own, -jnp.inf)
        logits = jnp.concatenate([s_sel.reshape(b_, nh, MOBA_QCHUNK, kk), s_own], axis=-1)
        p = jax.nn.softmax(logits, axis=-1).astype(vb.dtype)
        p_sel = p[..., :kk].reshape(b_, nh, MOBA_QCHUNK, topk, MOBA_BLOCK)
        p_own = p[..., kk:]
        return (jnp.einsum('bhqkp,bhqkpd->bhqd', p_sel, vs)
                + jnp.einsum('bhqp,bhpd->bhqd', p_own, vown))

    o = lax.map(chunk, (jnp.arange(nqc), qch))
    o = o.transpose(1, 0, 3, 2, 4).reshape(b_, s_, D_MODEL)
    return (o @ w_out).astype(h.dtype)

def swiglu(h, w13, w2):
    g, u = jnp.split(h @ w13, 2, axis=-1)
    return ((jax.nn.silu(g) * u) @ w2).astype(h.dtype)

def second_inputs(seed: int = 0) -> dict:
    key = jax.random.key(seed)
    ks = jax.random.split(key, 14)
    nrm = lambda k, shape, fan_in: jax.random.normal(k, shape, jnp.float32) * (fan_in ** -0.5)
    gain = lambda k, shape: 1.0 + 0.02 * jax.random.normal(k, shape, jnp.float32)
    return {
        "x": jax.random.normal(ks[0], (BATCH, SEQ, D_MODEL), jnp.float32),
        "norm_mix": gain(ks[1], (DEPTH_2, D_MODEL)),
        "norm_ffn": gain(ks[2], (DEPTH_2, D_MODEL)),
        "hgrn_w_in": nrm(ks[3], (N_A_LAYERS, D_MODEL, 2 * HGRN_FDIM + 2 * D_MODEL), D_MODEL),
        "hgrn_lb_logits": 1.0 + 0.1 * jax.random.normal(ks[4], (N_A_LAYERS + 1, HGRN_FDIM), jnp.float32),
        "hgrn_out_norm": gain(ks[5], (N_A_LAYERS, D_MODEL)),
        "hgrn_w_out": nrm(ks[6], (N_A_LAYERS, D_MODEL, D_MODEL), D_MODEL),
        "moba_w_in": nrm(ks[7], (N_B_LAYERS, D_MODEL, 3 * D_MODEL), D_MODEL),
        "moba_w_out": nrm(ks[8], (N_B_LAYERS, D_MODEL, D_MODEL), D_MODEL),
        "rel_bias_table": 0.5 * jax.random.normal(ks[9], (REL_BUCKETS, ATTN_HEADS), jnp.float32),
        "ffn_w13": nrm(ks[10], (DEPTH_2, D_MODEL, 2 * D_FF_2), D_MODEL),
        "ffn_w2": nrm(ks[11], (DEPTH_2, D_FF_2, D_MODEL), D_FF_2),
        "final_norm": gain(ks[12], (D_MODEL,)),
    }

def second_block(x, norm_mix, norm_ffn, hgrn_w_in, hgrn_lb_logits, hgrn_out_norm, hgrn_w_out,
              moba_w_in, moba_w_out, rel_bias_table, ffn_w13, ffn_w2, final_norm):
    lb_all = jnp.cumsum(jax.nn.softmax(hgrn_lb_logits.astype(jnp.float32), axis=0), axis=0)[:N_A_LAYERS]
    h = x
    for layer in range(DEPTH_2):
        y = rms_norm(h, norm_mix[layer])
        idx = layer // N_MIXERS
        if layer % N_MIXERS == 0:
            y = hgrn2_mixer(y, hgrn_w_in[idx], hgrn_w_out[idx], lb_all[idx], hgrn_out_norm[idx])
        else:
            y = moba_mixer(y, moba_w_in[idx], moba_w_out[idx], rel_bias_table)
        h = h + y
        h = h + swiglu(rms_norm(h, norm_ffn[layer]), ffn_w13[layer], ffn_w2[layer])
    return rms_norm(h, final_norm)


def setup_inputs(seed=0):
    out = dict(first_inputs(seed))
    for name, value in second_inputs(seed + 1).items():
        if name != "x":
            out[name + "_2"] = value
    return out


def reference(
    x, positions, norm_mix_g, w_in, idx_k_norm_g, q_a_norm_g, kv_a_norm_g, w_uq, w_uk, w_uv,
    w_branch_a, w_branch_b, w_out, norm_ffn_g, w_up, conv_w, conv_b, w_down, norm_final_g,
    norm_mix_2, norm_ffn_2, hgrn_w_in_2, hgrn_lb_logits_2, hgrn_out_norm_2, hgrn_w_out_2,
    moba_w_in_2, moba_w_out_2, rel_bias_table_2, ffn_w13_2, ffn_w2_2, final_norm_2,
):
    x = first_block(
        x, positions, norm_mix_g, w_in, idx_k_norm_g, q_a_norm_g, kv_a_norm_g, w_uq, w_uk, w_uv,
        w_branch_a, w_branch_b, w_out, norm_ffn_g, w_up, conv_w, conv_b, w_down, norm_final_g,
    )
    return second_block(
        x, norm_mix_2, norm_ffn_2, hgrn_w_in_2, hgrn_lb_logits_2, hgrn_out_norm_2, hgrn_w_out_2,
        moba_w_in_2, moba_w_out_2, rel_bias_table_2, ffn_w13_2, ffn_w2_2, final_norm_2,
    )


_drawn_inputs = setup_inputs


def setup_inputs(seed=0):
    import zlib

    import numpy as np

    out = dict(_drawn_inputs(seed))
    spreads = {}
    factors = {'idx_k_norm_g': 3.418,
     'q_a_norm_g': 8.0,
     'kv_a_norm_g': 8.0,
     'norm_ffn_g': 3.147,
     'conv_b': 5.811,
     'norm_mix_2': 3.91,
     'norm_ffn_2': 3.038,
     'hgrn_lb_logits_2': 6.549,
     'hgrn_out_norm_2': 4.887,
     'final_norm_2': 2.829}
    for name, (base, spread) in spreads.items():
        noise = np.random.default_rng([zlib.crc32(name.encode()), seed]).standard_normal(out[name].shape)
        drawn = base * np.exp(spread * noise) if base else spread * noise
        out[name] = __import__('jax').numpy.asarray(drawn.astype(out[name].dtype))
    for name, factor in factors.items():
        out[name] = (out[name] * factor).astype(out[name].dtype)
    return out
```

```python
from contextlib import ExitStack

import concourse.bass as bass
import numpy as np
from concourse import mybir

F32 = mybir.dt.float32
F32R = mybir.dt.float32r
I32 = mybir.dt.int32
ALU = mybir.AluOpType
ACT = mybir.ActivationFunctionType
AX_X = mybir.AxisListType.X

P = 128
S = 256
TT = S // P
D = 1024
DC = D // P
NF = 2816
PAIRS = NF // 256
HEADS = 8
KV_HEADS = 2
HD = 64
TOPK = min(256, S // 4)
BQ = 96
MOBA_SCALE = 128 ** -0.5
EPS = 1e-6
NBUCKET = 32
BIAS_LEN = 384

C_AQ, C_AK, C_AV, C_IQ, C_IK, C_IW, C_CQ, C_CKV, C_KR, C_G, C_END = (
    0, 512, 640, 768, 1280, 1344, 1352, 1608, 1736, 1768, 3816)
C_QB = 768

MASKED = 1.0e38
TAKEN = -3.0e38
FAR = 1.0e30

V_MIX1, V_FFN1, V_MIX2, V_FFN2, V_OUT, V_LB, V_CQ, V_CKV = 0, 8, 16, 32, 48, 56, 72, 74

K_ID, K_REV, K_BUCKET, K_FREQ, K_END = 0, 128, 256, 256 + BIAS_LEN, 256 + BIAS_LEN + 24
LEVELS = [64, 32, 16, 8, 4, 2, 1]


def shape_constants():
    c = np.zeros((P, K_END), np.float32)
    c[:, K_ID:K_ID + P] = np.eye(P)
    c[:, K_REV:K_REV + P] = np.eye(P)[::-1]
    dist = S - 1 - np.arange(BIAS_LEN)
    n = np.maximum(dist, 0)
    big = np.maximum(n, 16).astype(np.float32)
    large = 16 + (np.log(big / np.float32(16)) / np.float32(np.log(64)) * np.float32(16)).astype(np.int32)
    bucket = np.where(n < 16, n, np.minimum(large, 31))
    for j in range(BIAS_LEN):
        c[bucket[j] if dist[j] >= 0 else NBUCKET, K_BUCKET + j] = 1.0
    inv = [500000.0 ** (-2 * j / 16) for j in range(8)] + [500000.0 ** (-2 * j / 32) for j in range(16)]
    c[:, K_FREQ:K_END] = np.array(inv, np.float32)
    s, t = np.arange(P)[:, None], np.arange(P)[None, :]
    m = np.zeros((P, len(LEVELS) + 1, P), np.int32)
    for i, b in enumerate(LEVELS):
        m[:, i] = (s // (2 * b) == t // (2 * b)) & (s % (2 * b) < b) & (t % (2 * b) >= b)
    m[:, -1] = s == t
    return c, m


def plan_granules():
    g, at = [], {}

    def mark(name):
        at[name] = len(g)

    def token_blocks(name, layer, c0, c1):
        for c in range(c0, c1, 512):
            for k in (0, 4):
                g.append((name, layer, k, 4, c, min(512, c1 - c)))

    def feature_blocks(name, layer, c0, c1):
        for c in range(c0, c1, 256):
            g.append((name, layer, 0, DC, c, 256))

    def ffn(mark_name, up, down, layer):
        mark(mark_name)
        for p in range(PAIRS + 1):
            if p < PAIRS:
                g.append((up, layer, 0, DC, 256 * p, 256))
                g.append((up, layer, 0, DC, NF + 256 * p, 256))
            if p >= 1:
                g.append((down, layer, 2 * (p - 1), 2, 0, D))

    mark("in")
    token_blocks("w_in", 0, 0, C_G)
    mark("uq")
    g.append(("w_uq", 0, 0, 2, 0, 768))
    mark("uk")
    g.append(("w_uk", 0, 0, 1, 0, 512))
    mark("uv")
    g.append(("w_uv", 0, 0, 1, 0, 512))
    mark("gate")
    token_blocks("w_in", 0, C_G, C_END)
    mark("branch")
    for name in ("w_branch_a", "w_branch_b"):
        for c in (0, 512):
            g.append((name, 0, 0, 4, c, 512))
    mark("out")
    token_blocks("w_out", 0, 0, D)
    ffn("ffn0", "w_up", "w_down", 0)
    mark("hf")
    feature_blocks("hgrn_w_in_2", 0, 1024, 2048)
    mark("hq")
    feature_blocks("hgrn_w_in_2", 0, 0, 1024)
    mark("hi")
    token_blocks("hgrn_w_in_2", 0, 2048, 3072)
    mark("hg")
    token_blocks("hgrn_w_in_2", 0, 3072, 4096)
    mark("hout")
    token_blocks("hgrn_w_out_2", 0, 0, D)
    ffn("ffn1", "ffn_w13_2", "ffn_w2_2", 0)
    mark("mq")
    feature_blocks("moba_w_in_2", 0, 0, 2048)
    mark("mv")
    token_blocks("moba_w_in_2", 0, 2048, 3072)
    mark("mout")
    token_blocks("moba_w_out_2", 0, 0, D)
    ffn("ffn2", "ffn_w13_2", "ffn_w2_2", 1)
    mark("end")
    return g, at


def build(nc, a, out):
    granules, G = plan_granules()
    RING = 3
    GW = 2048

    with ExitStack() as ctx:
        def sb(name, shape, dt=F32):
            return ctx.enter_context(nc.sbuf_tensor(name, shape, dt))

        raw = sb("raw", [P, RING, GW])
        w_hi = sb("w_hi", [P, RING, GW], F32R)
        w_lo = sb("w_lo", [P, RING, GW], F32R)
        x_hi = sb("x_hi", [P, DC, S], F32R)
        x_lo = sb("x_lo", [P, DC, S], F32R)
        hid_hi = sb("hid_hi", [P, 4, S], F32R)
        hid_lo = sb("hid_lo", [P, 4, S], F32R)
        h = sb("h", [P, TT, D])
        xn = sb("xn", [P, TT, D])
        g_final = sb("g_final", [P, D])
        const = sb("const", [P, K_END])
        vcol = sb("vcol", [P, 3, 88])
        stat = sb("stat", [P, 160])
        work = sb("work", [P, 21760])
        ps = ctx.enter_context(nc.psum_tensor("ps", [P, 8, 512], F32))
        bias_scratch = nc.dram_tensor("bias_scratch", (HEADS, BIAS_LEN), F32, kind="Internal").ap()

        ident = const[:, K_ID:K_ID + P]
        reverse = const[:, K_REV:K_REV + P]

        def region(start, *dims, parts=P, dt=None):
            n = int(np.prod(dims))
            v = work[0:parts, start:start + n]
            names = "abcd"[:len(dims)]
            if len(dims) > 1:
                v = v.rearrange(f"p ({' '.join(names)}) -> p {' '.join(names)}", **dict(zip(names[1:], dims[1:])))
            return v

        proj = region(0, TT, C_G)
        gates = region(3536, TT, 2048)
        qi_T = region(7632, HEADS, S, parts=HD)
        qb_T = region(7632, HEADS, S, parts=BQ)
        qa_T = region(9680, HEADS, S, parts=HD)
        kb_T = region(11728, HEADS, S, parts=BQ)
        o_T = region(13776, DC, S)
        ka_T = region(15824, KV_HEADS, S, parts=HD)
        ki_T = region(16336, S, parts=HD)
        v_b = region(16592, TT, 512)
        prob = region(17616, 2, 2, S)
        prob_T = region(18640, 2, 2, TT, P)
        see = region(19664, TT, S)
        add_b = region(20176, TT, S)
        add_a = region(20688, TT, S)
        isc = region(21200, TT, S)
        vrow = region(9680, 3, P)
        posrow_i = region(11728, S).bitcast(I32)
        posrow = region(12240, S)
        pool_tmp = region(13776, 4, 160 * TT)
        g_ik = region(16592, HD)
        bias_row = region(17616, BIAS_LEN, parts=HEADS)

        conv = region(0, 2, 4, S)
        act_g = region(2048, 2, 512)
        hid = region(3072, 2, 512)

        Q = region(0, HEADS, S)
        K = region(2048, HEADS, S)
        CUM = region(4096, HEADS, S)
        E = region(6144, 2, HEADS, S)
        inp = region(10240, TT, D)
        ogate = region(12288, TT, D)
        pairs = region(14336, TT, HEADS, P)
        pairs_x = region(16384, HEADS, P)
        X = region(17408, HEADS, S)
        ones = region(19456, P)
        masks = region(19584, len(LEVELS) + 1, P).bitcast(I32)

        qm_T = region(0, HEADS, S)
        km_T = region(2048, HEADS, S)
        v_m = region(4096, TT, D)
        bias = region(6144, HEADS, S)
        probm = region(8192, 2, 2, S)
        probm_T = region(9216, 2, 2, TT, P)

        ssq = stat[:, 0:18]
        var = stat[:, 18:36]
        rstd = stat[:, 36:54]
        ssq6, var6, rstd6 = stat[:, 54:60], stat[:, 60:66], stat[:, 66:72]
        w_idx = stat[:, 72:88]
        top8 = stat[:, 88:104]
        rowmax = stat[:, 104:108]
        neg_max = stat[:, 108:112]
        row_sum = stat[:, 112:116]
        row_inv = stat[:, 116:120]
        lb = stat[:, 120:128]
        lb_rest = stat[:, 128:136]
        lb_tmp = stat[:, 136:152]
        minus_half = stat[:, 152:158]
        pos_col = stat[:, 158:160]
        trig = sb("trig", [P, 2, TT, 24])
        ang = sb("ang", [P, 4, TT * 24])
        pos_i = sb("pos_i", [P, TT], I32)
        table = sb("table", [NBUCKET + 1, HEADS])

        names = """x_in small_in pos_in const_in gain_in table_in masks_in final_in bias_out bias_in out_done
            setup vrow_T vcol_done bias_ps bias_sb table_set trig_ready see_ready
            hi_ready lo_ready products_done
            ssq_ready var_ready rstd_ready xn_ready xt_done xhi_ready xlo_ready h_added h_final
            proj_copied gate_copied ssq6_ready var6_ready rstd6_ready c_scaled idx_ready qk_ready kr_ready
            group_done group_copied dots_done relu_done relu_used mask_ready qb_copied qb_ready kv_copied
            scores_done scores_used neg_ready exp_done prob_ready probT_done probT_copied pv_done o_copied
            ohi_ready olo_ready
            conv_first conv_step conv_done mo_lo gated hid_ready hhi_ready hlo_ready
            f_sig f_ready logf_done cum_ready q_ready e_ready e_exp x_ready pairs_done pairs_used
            cross_done cross_copied inp_copied og_copied o_done lb_ready
            mqk_copied mv_copied mo_hi dve_step act_step pool_step""".split()
        s = {n: ctx.enter_context(nc.semaphore(n)) for n in names}
        raw_in = [ctx.enter_context(nc.semaphore(f"raw_in{i}")) for i in range(RING)]
        block = ctx.enter_context(nc.Block())

        def granule_views(n):
            name, layer, k0, kc, c0, cols = granules[n]
            dst = raw[:, n % RING, 0:kc * cols].rearrange("p (c n) -> p c n", c=kc)
            return dst, cols

        def f32(ap):
            return ap.bitcast(F32)

        class Chain:

            def __init__(self, eng, sem):
                self.eng, self.sem, self.n = eng, sem, 0

            def __call__(self, ins):
                self.n += 1
                ins.then_inc(self.sem, 1)
                self.eng.wait_ge(self.sem, self.n)

        @block.sync
        def _(sp):
            def load(n, i=None, step=None):
                name, layer, k0, kc, c0, cols = granules[n]
                more = 0 if i is None else 6 * i
                w = a[name][layer]
                if name in ("w_uq", "w_uk", "w_uv"):
                    w = w.rearrange("r h d -> r (h d)")
                if i is None:
                    src = w[k0 * P:(k0 + kc) * P, c0:c0 + cols]
                elif step == "columns":
                    src = w[k0 * P:(k0 + kc) * P, bass.ds(sp.snap(i * 512 + c0), cols)]
                else:
                    src = w[bass.ds(sp.snap(i * 512 + k0 * P), kc * P), c0:c0 + cols]
                dst, _ = granule_views(n)
                src = src.rearrange("(c p) n -> p c n", p=P)
                if n >= RING:
                    sp.wait_ge(s["lo_ready"], more + (n - RING + 1))
                sp.dma_start(dst, src).then_inc(raw_in[n % RING], 16)

            def load_ffn(n0):
                for n in range(n0, n0 + 5):
                    load(n)
                with sp.Fori(0, 4) as i:
                    for j in range(6):
                        load(n0 + 5 + j, i, "columns" if j % 3 < 2 else "rows")
                for n in range(n0 + 29, n0 + 33):
                    load(n)

            sp.dma_start(h[:, :, :], a["x"][0].rearrange("(t p) d -> p t d", p=P)).then_inc(s["x_in"], 16)
            for n in range(G["ffn0"]):
                load(n)
            load_ffn(G["ffn0"])
            for n in range(G["hf"], G["ffn1"]):
                load(n)
            load_ffn(G["ffn1"])
            for n in range(G["mq"], G["ffn2"]):
                load(n)
            load_ffn(G["ffn2"])
            sp.wait_ge(s["h_final"], 4)
            sp.dma_start(out[0].rearrange("(t p) d -> p t d", p=P), h[:, :, :]).then_inc(s["out_done"], 16)
            sp.wait_ge(s["out_done"], 16)

        @block.gpsimd
        def _(pool):
            then = Chain(pool, s["pool_step"])

            def power(src, dst, ready, n, signal):
                w = src.shape[1]
                pool.wait_ge(ready, n)
                pool.tensor_tensor(dst, src, minus_half[:, 0:w], ALU.pow).then_inc(signal, 1)

            pool.wait_ge(s["setup"], 2)
            power(var[:, 0:2], rstd[:, 0:2], s["var_ready"], 1, s["rstd_ready"])
            power(var6, rstd6, s["var6_ready"], 1, s["rstd6_ready"])
            pool.wait_ge(s["trig_ready"], 1)
            pool.wait_ge(s["proj_copied"], 4)

            def rotate(x, heads, width, off, half, freq):
                v = x.rearrange("p t (h w) -> p t h w", w=width)
                x1, x2 = v[:, :, :, off:off + half], v[:, :, :, off + half:off + 2 * half]
                n = TT * heads * half
                t = [pool_tmp[:, i, 0:n].rearrange("p (t h w) -> p t h w", t=TT, w=half) for i in range(4)]
                cos = trig[:, 0, :, freq:freq + half].unsqueeze(2).broadcast_to((P, TT, heads, half))
                sin = trig[:, 1, :, freq:freq + half].unsqueeze(2).broadcast_to((P, TT, heads, half))
                pool.tensor_tensor(t[0], x1, cos, ALU.mult)
                pool.tensor_tensor(t[1], x2, sin, ALU.mult)
                pool.tensor_tensor(t[2], x1, sin, ALU.mult)
                then(pool.tensor_tensor(t[3], x2, cos, ALU.mult))
                pool.tensor_tensor(x1, t[0], t[1], ALU.subtract)
                return pool.tensor_tensor(x2, t[2], t[3], ALU.add)

            rotate(proj[:, :, C_AQ:C_AV], 10, HD, 0, 8, 0).then_inc(s["qk_ready"], 1)
            pool.wait_ge(s["qk_ready"], 1)
            rotate(proj[:, :, C_KR:C_G], 1, 32, 0, 16, 8).then_inc(s["kr_ready"], 1)
            pool.wait_ge(s["qb_copied"], 1)
            pool.wait_ge(s["kr_ready"], 1)
            rotate(proj[:, :, C_QB:C_QB + 768], HEADS, BQ, HD, 16, 8).then_inc(s["qb_ready"], 1)
            for m in range(1, 4):
                power(var[:, 2 * m:2 * m + 2], rstd[:, 2 * m:2 * m + 2], s["var_ready"], m + 1, s["rstd_ready"])
            pool.wait_ge(s["cum_ready"], 1)
            cum = CUM.rearrange("p h t -> p (h t)")
            for lv, b in enumerate(LEVELS):
                if lv >= 2:
                    pool.wait_ge(s["x_ready"], 2 * (lv - 1))
                c = cum.rearrange("p (g w) -> p g w", w=2 * b)
                e = E[:, lv % 2].rearrange("p h t -> p (h t)").rearrange("p (g w) -> p g w", w=2 * b)
                mid = c[:, :, b - 1:b].broadcast_to((P, HEADS * S // (2 * b), b))
                pool.tensor_tensor(e[:, :, b:2 * b], c[:, :, b:2 * b], mid, ALU.subtract)
                pool.tensor_tensor(e[:, :, 0:b], mid, c[:, :, 0:b], ALU.subtract).then_inc(s["e_ready"], 1)
            pool.wait_ge(s["x_ready"], 2 * (len(LEVELS) - 1))
            e = E[:, len(LEVELS) % 2]
            pool.tensor_copy(e[:, :, P:S], CUM[:, :, P:S])
            pool.tensor_tensor(e[:, :, 0:P], CUM[:, :, P - 1:P].broadcast_to((P, HEADS, P)), CUM[:, :, 0:P],
                               ALU.subtract).then_inc(s["e_ready"], 1)
            for m in range(4, 9):
                power(var[:, 2 * m:2 * m + 2], rstd[:, 2 * m:2 * m + 2], s["var_ready"], m + 1, s["rstd_ready"])

        @block.scalar
        def _(act):
            then = Chain(act, s["act_step"])

            def hi(n, i=None):
                more, turns = (0, 0) if i is None else (6 * i, 32 * i)
                _, _, _, kc, _, cols = granules[n]
                act.wait_ge(raw_in[n % RING], turns + 16 * (n // RING + 1))
                if n >= RING:
                    act.wait_ge(s["products_done"], more + (n - RING + 1))
                act.activation(w_hi[:, n % RING, 0:kc * cols], raw[:, n % RING, 0:kc * cols], ACT.Copy).then_inc(s["hi_ready"], 1)

            def hi_of(*ns):
                for n in ns:
                    hi(n)

            def operand_hi(k, gain):
                for c in range(DC):
                    if c % 2 == 0:
                        act.wait_ge(s["xt_done"], 4 * k + c // 2 + 1)
                    act.activation(x_hi[:, c, :], ps[:, c // 2, 256 * (c % 2):256 * (c % 2) + 256], ACT.Copy,
                                   scale=1.0 if gain is None else vcol[:, 0, gain + c:gain + c + 1]).then_inc(s["xhi_ready"], 1)

            def squares(m, src):
                for t in range(TT):
                    ins = act.activation(xn[:, t, :], src(t), ACT.Square, accum_out=ssq[:, 2 * m + t:2 * m + t + 1])
                ins.then_inc(s["ssq_ready"], 1)

            def units(first, count, scale, psum_scores, copy_o, extra):
                def exps(u):
                    act.wait_ge(s["neg_ready"], u + 1)
                    for j in range(2):
                        src, dst = psum_scores(u, j)
                        ins = act.activation(dst, src, ACT.Exp, scale=scale(u),
                                             bias=neg_max[:, 2 * (u % 2) + j:2 * (u % 2) + j + 1],
                                             accum_out=row_sum[:, 2 * (u % 2) + j:2 * (u % 2) + j + 1])
                    ins.then_inc(s["exp_done"], 1)

                exps(first)
                for u in range(first, first + count):
                    if u + 1 < first + count:
                        exps(u + 1)
                    act.wait_ge(s["probT_done"], u + 1)
                    n, dst = prob_T_of(u)
                    act.activation(dst, ps[:, u % 2, 0:n], ACT.Copy).then_inc(s["probT_copied"], 1)
                    act.wait_ge(s["pv_done"], u + 1)
                    copy_o(u)
                    extra(u)

            def prob_T_of(u):
                if u < 16:
                    return 512, prob_T[:, u % 2].rearrange("p a b c -> p (a b c)")
                n = 256 if (u - 16) % 2 == 0 else 512
                return n, probm_T[:, u % 2].rearrange("p a b c -> p (a b c)")[:, 0:n]

            act.dma_start(const[:, :], a["const"]).then_inc(s["const_in"], 16)
            act.dma_start(pos_i[:, :], a["positions"][0].rearrange("(t p) -> p t", p=P), allow_slow_non_contiguous=True).then_inc(s["pos_in"], 16)
            act.dma_start(posrow_i, a["positions"][0].partition_broadcast(P)).then_inc(s["pos_in"], 16)

            for r, name in ((V_MIX1, "norm_mix_g"), (V_FFN1, "norm_ffn_g"), (V_MIX2, "norm_mix_2"), (V_FFN2, "norm_ffn_2"),
                            (V_OUT, "hgrn_out_norm_2"), (V_LB, "hgrn_lb_logits_2"), (V_CQ, "q_a_norm_g"), (V_CKV, "kv_a_norm_g")):
                v = a[name]
                v = v.rearrange("l (c p) -> (l c) p", p=P)
                act.dma_start(vrow[r:r + v.shape[0], 0, :], v).then_inc(s["small_in"], 16)
            taps = a["conv_w"][0].rearrange("j (c p) -> j c p", p=P)
            for j in range(3):
                act.dma_start(vrow[44 * (j % 2):44 * (j % 2) + 44, 1 + j // 2, :], taps[j]).then_inc(s["small_in"], 16)
            act.dma_start(vrow[44:88, 2, :], a["conv_b"][0].rearrange("(c p) -> c p", p=P)).then_inc(s["small_in"], 16)
            act.dma_start(g_ik, a["idx_k_norm_g"][0].partition_broadcast(P)).then_inc(s["gain_in"], 16)
            act.dma_start(table[0:NBUCKET, :], a["rel_bias_table_2"]).then_inc(s["table_in"], 16)
            act.dma_start(g_final[:, :], a["norm_final_g"].partition_broadcast(P)).then_inc(s["final_in"], 16)

            act.wait_ge(s["x_in"], 16)
            squares(0, lambda t: h[:, t, :])
            hi_of(0, 1, 2)
            act.wait_ge(s["setup"], 3)
            act.activation(trig[:, 1].rearrange("p t f -> p (t f)"), ang[:, 0, :], ACT.Sin)
            act.activation(trig[:, 0].rearrange("p t f -> p (t f)"), ang[:, 1, :], ACT.Sin).then_inc(s["trig_ready"], 1)
            act.wait_ge(s["vrow_T"], 1)
            act.activation(vcol[:, 0, 0:75], ps[:, 4, 0:75], ACT.Copy)
            act.activation(vcol[:, 1:3, :].rearrange("p g n -> p (g n)"), ps[:, 4, 88:264], ACT.Copy).then_inc(s["vcol_done"], 1)
            act.wait_ge(s["bias_ps"], 1)
            act.activation(bias_row[:, :], ps[0:HEADS, 5, 0:BIAS_LEN], ACT.Copy).then_inc(s["bias_sb"], 1)
            act.wait_ge(s["bias_sb"], 1)
            act.dma_start(bias_scratch, bias_row[:, :]).then_inc(s["bias_out"], 16)
            act.wait_ge(s["vcol_done"], 1)
            operand_hi(0, V_MIX1)

            def copy_proj(b):
                c0, c1 = 512 * b, min(512 * b + 512, C_G)
                act.wait_ge(s["products_done"], 2 * b + 2)
                bank = 4 + 2 * (b % 2)
                act.activation(proj[:, :, c0:c1], ps[:, bank:bank + 2, 0:c1 - c0], ACT.Copy).then_inc(s["proj_copied"], 1)

            hi_of(3, 4)
            copy_proj(0)
            hi_of(5, 6)
            copy_proj(1)
            hi_of(7, 8)
            copy_proj(2)
            hi_of(9)
            copy_proj(3)
            hi_of(10)
            act.wait_ge(s["proj_copied"], 4)
            for i, (c0, n) in enumerate(((C_IK, HD), (C_CQ, 256), (C_CKV, P))):
                for t in range(TT):
                    ins = act.activation(xn[:, t, 256 * i:256 * i + n], proj[:, t, c0:c0 + n], ACT.Square, accum_out=ssq6[:, 2 * i + t:2 * i + t + 1])
            ins.then_inc(s["ssq6_ready"], 1)
            act.wait_ge(s["rstd6_ready"], 1)
            for i, (c0, n) in ((1, (C_CQ, 256)), (2, (C_CKV, P))):
                for t in range(TT):
                    ins = act.activation(proj[:, t, c0:c0 + n], proj[:, t, c0:c0 + n], ACT.Copy, scale=rstd6[:, 2 * i + t:2 * i + t + 1])
            ins.then_inc(s["c_scaled"], 1)

            def group(n, dst, src, last=True, **kw):
                act.wait_ge(s["group_done"], n + 1)
                ins = act.activation(dst, src, ACT.Copy, **kw)
                if last:
                    ins.then_inc(s["group_copied"], 1)

            group(0, ki_T, ps[0:HD, 0, 0:S])
            for j in range(4):
                group(1 + j, qi_T[:, 2 * j:2 * j + 2, :].rearrange("p a b -> p (a b)"), ps[0:HD, (1 + j) % 2, :])

            def relus(t):
                for j in range(4):
                    n = 4 * t + j
                    act.wait_ge(s["dots_done"], n + 1)
                    if n >= 2:
                        act.wait_ge(s["relu_used"], n - 1)
                    act.activation(prob[:, n % 2].rearrange("p a b -> p (a b)"), ps[:, 2 + n % 2, :], ACT.Relu,
                                   scale=HD ** -0.5).then_inc(s["relu_done"], 1)

            for c in range(3):
                act.wait_ge(s["group_done"], 6 + c // 2)
                act.activation(hid_hi[:, c, :], ps[:, (5 + c // 2) % 2, 256 * (c % 2):256 * (c % 2) + 256], ACT.Copy,
                               scale=vcol[:, 0, V_CQ + c:V_CQ + c + 1]).then_inc(s["hhi_ready"], 1)
            group(7, kb_T[HD:BQ, :, :], ps[HD:BQ, 1, 0:S].unsqueeze(1).broadcast_to((BQ - HD, HEADS, S)))
            group(8, ka_T.rearrange("p a b -> p (a b)"), ps[0:HD, 0, :])
            for j in range(4):
                group(9 + j, qa_T[:, 2 * j:2 * j + 2, :].rearrange("p a b -> p (a b)"), ps[0:HD, (9 + j) % 2, :])
            act.wait_ge(s["bias_out"], 16)
            relus(0)
            relus(1)
            act.wait_ge(s["products_done"], G["uq"] + 1)
            act.activation(proj[:, 0, C_QB:C_QB + 768].rearrange("p (a b) -> p a b", a=2), ps[:, 4:6, 0:384], ACT.Copy)
            act.activation(proj[:, 1, C_QB:C_QB + 768].rearrange("p (a b) -> p a b", a=2), ps[:, 6:8, 0:384], ACT.Copy).then_inc(s["qb_copied"], 1)
            act.wait_ge(s["products_done"], G["uv"] + 1)
            for bank in range(2):
                src = ps[:, bank, :].rearrange("p (a b) -> p a b", a=2)
                act.activation(kb_T[0:HD, 4 * bank:4 * bank + 3:2, :], src[0:HD], ACT.Copy)
                act.activation(kb_T[0:HD, 4 * bank + 1:4 * bank + 4:2, :], src[HD:P], ACT.Copy)
            act.activation(v_b, ps[:, 2:4, :], ACT.Copy).then_inc(s["kv_copied"], 1)
            for j in range(4):
                group(13 + j, qb_T[:, 2 * j:2 * j + 2, :].rearrange("p a b -> p (a b)"), ps[0:BQ, (13 + j) % 2, :])
            g0 = G["gate"]
            hi_of(g0, g0 + 1, g0 + 2)

            def scores1(u, j):
                return prob[:, u % 2, j, :], prob[:, u % 2, j, :]

            def copy_o1(u):
                t, j = u % 2, (u % 8) // 2
                chunk = (4 if u < 8 else 0) + j
                act.activation(o_T[:, chunk, P * t:P * t + P], ps[:, 4 + u % 2, 0:P], ACT.Copy).then_inc(s["o_copied"], 1)

            def gate_work(u):
                if u % 2 == 1:
                    hi(g0 + 3 + u // 2)
                if u % 4 == 2:
                    b = u // 4
                    act.wait_ge(s["products_done"], g0 + 2 * b + 2)
                    act.activation(gates[:, :, 512 * b:512 * b + 512], ps[:, 6:8, :], ACT.Sigmoid).then_inc(s["gate_copied"], 1)

            units(0, 16, lambda u: (BQ ** -0.5 if u < 8 else HD ** -0.5), scores1, copy_o1, gate_work)
            for c in range(0, DC, 2):
                if c == 0:
                    act.wait_ge(s["products_done"], G["branch"])
                    act.wait_ge(s["o_copied"], 16)
                act.activation(x_hi[:, c:c + 2, :], o_T[:, c:c + 2, :], ACT.Copy).then_inc(s["ohi_ready"], 1)
            b0 = G["branch"]
            hi_of(b0 + 3, b0 + 4, b0 + 5, b0 + 6)
            operand_hi(1, None)

            def out_squares(m, adds):
                act.wait_ge(s["h_added"], adds)
                squares(m, lambda t: h[:, t, :])

            hi_of(b0 + 7)
            f0 = G["ffn0"]
            hi_of(f0, f0 + 1, f0 + 2)
            out_squares(1, 2)
            operand_hi(2, V_FFN1)

            def ffn(n0, f, tail):
                def post(p, n_gate, i=None):
                    par = p % 2
                    more = 0 if i is None else 2 * i
                    done = 0 if i is None else 6 * i
                    P0 = PAIRS * f + p
                    if f == 0:
                        act.wait_ge(s["products_done"], done + (n_gate + 1))
                        for ft in range(4):
                            if ft == 2:
                                act.wait_ge(s["products_done"], done + (n_gate + 2))
                            col = 22 * (ft // 2) + 2 * p + ft % 2
                            c = col if i is None else i * 4 + col
                            last = vcol[:, 2, c:c + 1] if i is None else vcol[:, 2, bass.ds(c, 1)]
                            bias_c = vcol[:, 2, 44 + c:45 + c] if i is None else vcol[:, 2, bass.ds(c + 44, 1)]
                            act.activation(conv[:, par, ft, :], ps[:, 2 * par + ft // 2, 256 * (ft % 2):256 * (ft % 2) + 256],
                                           ACT.Identity, scale=last, bias=bias_c).then_inc(s["conv_first"], 1)
                        act.wait_ge(s["conv_done"], more + P0 + 1)
                        act.activation(act_g[:, par, :], conv[:, par, 0:2, :].rearrange("p a b -> p (a b)"), ACT.Silu).then_inc(s["gated"], 1)
                    else:
                        act.wait_ge(s["products_done"], done + (n_gate + 1))
                        act.activation(act_g[:, par, :], ps[:, 2 * par, :], ACT.Silu).then_inc(s["gated"], 1)

                def post_hi(p, i=None):
                    par = p % 2
                    P0 = PAIRS * f + p
                    more = 0 if i is None else 2 * i
                    act.wait_ge(s["hid_ready"], more + P0 + 1)
                    act.activation(hid_hi[:, 2 * par:2 * par + 2, :].rearrange("p a b -> p (a b)"), hid[:, par, :],
                                   ACT.Copy).then_inc(s["hhi_ready"], 1)

                hi(n0 + 3)
                post(0, n0)
                hi(n0 + 4)
                post_hi(0)
                hi(n0 + 5)
                post(1, n0 + 2)
                hi(n0 + 6)
                post_hi(1)
                hi(n0 + 7)
                with act.Fori(0, 4) as i:
                    for q in range(2):
                        hi(n0 + 8 + 3 * q, i)
                        post(2 + q, n0 + 5 + 3 * q, i)
                        hi(n0 + 9 + 3 * q, i)
                        post_hi(2 + q, i)
                        hi(n0 + 10 + 3 * q, i)
                n1 = n0 + 29
                hi_next(n1 + 3)
                post(10, n1)
                hi_next(n1 + 4)
                post_hi(10)
                hi_next(n1 + 5)
                tail(n1 + 6)

            def hi_next(n):
                if n < G["end"]:
                    hi(n)

            ffn(f0, 0, hi_next)
            out_squares(2, 4)
            act.wait_ge(s["h_final"], 2)
            act.dma_start(g_final[:, :], a["final_norm_2"].partition_broadcast(P)).then_inc(s["final_in"], 16)
            act.dma_start(masks, a["pair_masks"]).then_inc(s["masks_in"], 16)
            squares(3, lambda t: h[:, t, :])
            lbl = [vcol[:, 0, V_LB + 8 * r:V_LB + 8 * r + 8] for r in range(2)]
            act.wait_ge(s["lb_ready"], 1)
            act.activation(lb_tmp, lb_tmp, ACT.Exp).then_inc(s["lb_ready"], 1)
            operand_hi(3, V_MIX2)
            nf = G["hf"]

            for j in range(4):
                act.wait_ge(s["products_done"], nf + j + 1)
                act.activation(K[:, 2 * j:2 * j + 2, :].rearrange("p a b -> p (a b)"), ps[:, j, :], ACT.Sigmoid).then_inc(s["f_sig"], 1)
                hi(nf + 3 + j)
            for j in range(4):
                act.wait_ge(s["products_done"], nf + 5 + j)
                act.activation(Q[:, 2 * j:2 * j + 2, :].rearrange("p a b -> p (a b)"), ps[:, 4 + j, :], ACT.Silu).then_inc(s["q_ready"], 1)
                hi(nf + 7 + j)
            act.wait_ge(s["f_ready"], 1)
            act.activation(CUM.rearrange("p a b -> p (a b)"), E[:, 0].rearrange("p a b -> p (a b)"), ACT.Ln).then_inc(s["logf_done"], 1)

            def exp_level(lv):
                act.wait_ge(s["e_ready"], lv + 1)
                e = E[:, lv % 2].rearrange("p a b -> p (a b)")
                act.activation(e, e, ACT.Exp).then_inc(s["e_exp"], 1)

            def copy_block(b):
                bank = 4 + 2 * (b % 2)
                act.wait_ge(s["products_done"], nf + 8 + 2 * b + 2)
                c = 512 * (b % 2)
                dst = (inp if b < 2 else ogate)[:, :, c:c + 512]
                act.activation(dst, ps[:, bank:bank + 2, :], ACT.Copy if b < 2 else ACT.Sigmoid).then_inc(
                    s["inp_copied"] if b < 2 else s["og_copied"], 1)

            nh = nf + 8
            exp_level(0)
            hi_of(nh + 3)
            exp_level(1)
            copy_block(0)
            hi_of(nh + 4, nh + 5)
            exp_level(2)
            copy_block(1)
            hi_of(nh + 6, nh + 7)
            exp_level(3)
            copy_block(2)
            hi_of(nh + 8)
            exp_level(4)
            copy_block(3)
            hi_of(nh + 9, nh + 10)
            for lv in range(5, 8):
                exp_level(lv)
            act.wait_ge(s["cross_done"], 1)
            act.activation(pairs_x, ps[:, 4:6, :].rearrange("p a (b c) -> p (a b) c", c=P), ACT.Copy).then_inc(s["cross_copied"], 1)
            act.wait_ge(s["o_done"], 1)
            for t in range(TT):
                ins = act.activation(xn[:, t, :].rearrange("p (a b) -> p a b", a=2), ps[:, 2 * t:2 * t + 2, :], ACT.Square,
                                     accum_out=ssq[:, 8 + t:9 + t])
            ins.then_inc(s["ssq_ready"], 1)
            operand_hi(4, V_OUT)
            no = G["hout"]
            hi_next(no + 3)
            hi_next(no + 4)
            hi_next(no + 5)
            hi_next(no + 6)
            out_squares(5, 6)
            operand_hi(5, V_FFN2)
            ffn(G["ffn1"], 1, hi_next)
            out_squares(6, 8)
            act.wait_ge(s["bias_out"], 16)
            skew = bass.AP(bias_scratch.tensor, 0, [[1, P], [BIAS_LEN, HEADS], [1, S]])
            act.dma_start(bias, skew).then_inc(s["bias_in"], 16)
            operand_hi(6, V_MIX2 + 8)
            nm = G["mq"]
            for j in range(8):
                act.wait_ge(s["products_done"], nm + j + 1)
                dst = (qm_T if j < 4 else km_T)[:, 2 * (j % 4):2 * (j % 4) + 2, :].rearrange("p a b -> p (a b)")
                act.activation(dst, ps[:, j % 4, :], ACT.Copy, scale=MOBA_SCALE if j < 4 else 1.0).then_inc(s["mqk_copied"], 1)
                hi(nm + 3 + j)
            for b in range(2):
                act.wait_ge(s["products_done"], nm + 8 + 2 * b + 2)
                act.activation(v_m[:, :, 512 * b:512 * b + 512], ps[:, 4 + 2 * b:6 + 2 * b, :], ACT.Copy).then_inc(s["mv_copied"], 1)
                hi(nm + 11 + 2 * b)
                hi(nm + 12 + 2 * b)

            def scores2(u, j):
                n = P if (u - 16) % 2 == 0 else S
                return ps[:, 2 + u % 2, n * j:n * j + n], probm[:, u % 2, j, 0:n]

            def copy_o2(u):
                t, j = (u - 16) % 2, (u - 16) // 2
                act.activation(x_hi[:, 2 * j:2 * j + 2, P * t:P * t + P],
                               ps[:, 4 + u % 2, 0:256].rearrange("p (a b) -> p a b", a=2), ACT.Copy).then_inc(s["mo_hi"], 1)

            units(16, 8, lambda u: 1.0, scores2, copy_o2, lambda u: None)
            no = G["mout"]
            hi_of(no + 3, no + 4, no + 5, no + 6)
            out_squares(7, 10)
            operand_hi(7, V_FFN2 + 8)
            ffn(G["ffn2"], 2, hi_next)
            out_squares(8, 12)

        @block.vector
        def _(dve):
            then = Chain(dve, s["dve_step"])

            def lo(n, i=None):
                _, _, _, kc, _, cols = granules[n]
                sl = slice(0, kc * cols)
                dve.wait_ge(s["hi_ready"], (n + 1) if i is None else 6 * i + (n + 1))
                dve.tensor_tensor(w_lo[:, n % RING, sl], raw[:, n % RING, sl], f32(w_hi[:, n % RING, sl]), ALU.subtract).then_inc(s["lo_ready"], 1)

            def lo_of(*ns):
                for n in ns:
                    lo(n)

            def operand_lo(k, gain):
                for c in range(DC):
                    dve.wait_ge(s["xhi_ready"], DC * k + 2 * (c // 2) + 2)
                    dve.scalar_tensor_tensor(x_lo[:, c, :], ps[:, c // 2, 256 * (c % 2):256 * (c % 2) + 256],
                                             1.0 if gain is None else vcol[:, 0, gain + c:gain + c + 1], f32(x_hi[:, c, :]),
                                             ALU.mult, ALU.subtract).then_inc(s["xlo_ready"], 1)

            def variance(m):
                dve.wait_ge(s["ssq_ready"], m + 1)
                dve.tensor_scalar(var[:, 2 * m:2 * m + 2], ssq[:, 2 * m:2 * m + 2], 1.0 / D, EPS, ALU.mult, ALU.add).then_inc(s["var_ready"], 1)

            def normalize(m):
                variance(m)
                dve.wait_ge(s["rstd_ready"], m + 1)
                for t in range(TT):
                    ins = dve.tensor_scalar(xn[:, t, :], h[:, t, :], rstd[:, 2 * m + t:2 * m + t + 1], None, ALU.mult)
                ins.then_inc(s["xn_ready"], 1)

            def add_residual(n_last):
                for c in range(2):
                    dve.wait_ge(s["products_done"], n_last[c] + 1)
                    dve.tensor_tensor(h[:, :, 512 * c:512 * c + 512], ps[:, 4 + 2 * c:6 + 2 * c, :], h[:, :, 512 * c:512 * c + 512],
                                      ALU.add).then_inc(s["h_added"], 1)

            dve.memset(minus_half, -0.5).then_inc(s["setup"], 1)
            dve.memset(table[NBUCKET:NBUCKET + 1, :], -FAR).then_inc(s["setup"], 1)
            dve.wait_ge(s["pos_in"], 32)
            then(dve.tensor_copy(pos_col, pos_i[:, :]))
            dve.wait_ge(s["const_in"], 16)
            freq = const[:, K_FREQ:K_END]
            A0, A1, A2 = ang[:, 0, :], ang[:, 1, :], ang[:, 2, :]
            for t in range(TT):
                ins = dve.tensor_scalar(ang[:, 0, 24 * t:24 * t + 24], freq, pos_col[:, t:t + 1], None, ALU.mult)
            then(ins)
            turn = 2 * np.pi
            for unit in (4096.0, 1.0):
                full = turn * unit
                parts, rest = [], full
                for bits in (12, 12, 24):
                    e = int(np.floor(np.log2(abs(rest)))) - (bits - 1)
                    q = float(np.round(rest / 2.0 ** e) * 2.0 ** e)
                    parts.append(q)
                    rest -= q
                then(dve.tensor_scalar(A1, A0, float(np.float32(1 / full)), 12582912.0, ALU.mult, ALU.add))
                then(dve.tensor_scalar(A1, A1, 12582912.0, None, ALU.subtract))
                for q in parts:
                    then(dve.scalar_tensor_tensor(A0, A1, -q, A0, ALU.mult, ALU.add))
            then(dve.tensor_scalar(A0, A0, 3.1415925, -3.1415925, ALU.min, ALU.max))
            then(dve.tensor_scalar(A1, A0, -1.0, None, ALU.mult))
            then(dve.tensor_tensor(A1, A1, A0, ALU.min))
            dve.tensor_scalar(A1, A1, float(np.pi / 2), None, ALU.add).then_inc(s["setup"], 1)
            lo_of(0, 1, 2)
            then(dve.tensor_copy(posrow, posrow_i))
            for t in range(TT):
                ins = dve.tensor_scalar(see[:, t, :], posrow, pos_col[:, t:t + 1], None, ALU.is_le)
            then(ins)
            then(dve.tensor_scalar(add_b, see, -1.0, FAR, ALU.add, ALU.mult))
            normalize(0)
            operand_lo(0, V_MIX1)
            lo_of(*range(3, 11))
            dve.wait_ge(s["ssq6_ready"], 1)
            dve.tensor_scalar(var6[:, 0:2], ssq6[:, 0:2], 1.0 / HD, EPS, ALU.mult, ALU.add)
            dve.tensor_scalar(var6[:, 2:4], ssq6[:, 2:4], 1.0 / 256, EPS, ALU.mult, ALU.add)
            dve.tensor_scalar(var6[:, 4:6], ssq6[:, 4:6], 1.0 / P, EPS, ALU.mult, ALU.add).then_inc(s["var6_ready"], 1)
            dve.tensor_scalar(w_idx.rearrange("p (t h) -> p t h", t=TT), proj[:, :, C_IW:C_IW + HEADS], HEADS ** -0.5, None, ALU.mult)
            dve.wait_ge(s["rstd6_ready"], 1)
            dve.wait_ge(s["gain_in"], 16)
            for t in range(TT):
                ins = dve.scalar_tensor_tensor(proj[:, t, C_IK:C_IK + HD], proj[:, t, C_IK:C_IK + HD], rstd6[:, t:t + 1], g_ik,
                                               ALU.mult, ALU.mult)
            then(ins)
            dve.wait_ge(s["trig_ready"], 1)

            def rotate(x, heads, width, off, half, freq0, tmp):
                v = x.rearrange("p t (h w) -> p t h w", w=width)
                n = TT * heads * half
                t4 = [tmp[:, i, 0:n].rearrange("p (t h w) -> p t h w", t=TT, w=half) for i in range(4)]
                x1, x2 = v[:, :, :, off:off + half], v[:, :, :, off + half:off + 2 * half]
                cos = trig[:, 0, :, freq0:freq0 + half].unsqueeze(2).broadcast_to((P, TT, heads, half))
                sin = trig[:, 1, :, freq0:freq0 + half].unsqueeze(2).broadcast_to((P, TT, heads, half))
                dve.tensor_tensor(t4[0], x1, cos, ALU.mult)
                dve.tensor_tensor(t4[1], x2, sin, ALU.mult)
                dve.tensor_tensor(t4[2], x1, sin, ALU.mult)
                then(dve.tensor_tensor(t4[3], x2, cos, ALU.mult))
                dve.tensor_tensor(x1, t4[0], t4[1], ALU.subtract)
                return dve.tensor_tensor(x2, t4[2], t4[3], ALU.add)

            tmp_i = region(7632, 4, 160)
            rotate(proj[:, :, C_IQ:C_IW], 9, HD, 0, 8, 0, tmp_i).then_inc(s["idx_ready"], 1)
            for c in range(3):
                dve.wait_ge(s["hhi_ready"], 2 if c < 2 else 3)
                ins = dve.scalar_tensor_tensor(hid_lo[:, c, :], ps[:, (5 + c // 2) % 2, 256 * (c % 2):256 * (c % 2) + 256],
                                               vcol[:, 0, V_CQ + c:V_CQ + c + 1], f32(hid_hi[:, c, :]), ALU.mult, ALU.subtract)
                ins.then_inc(s["hlo_ready"], 1)
            for n in range(8):
                t, j = n // 4, n % 4
                dve.wait_ge(s["relu_done"], n + 1)
                for hh in range(2):
                    w = w_idx[:, 8 * t + 2 * j + hh:8 * t + 2 * j + hh + 1]
                    if j == 0 and hh == 0:
                        ins = dve.tensor_scalar(isc[:, t, :], prob[:, n % 2, 0, :], w, None, ALU.mult)
                    else:
                        ins = dve.scalar_tensor_tensor(isc[:, t, :], prob[:, n % 2, hh, :], w, isc[:, t, :], ALU.mult, ALU.add)
                    if hh == 0:
                        then(ins)
                ins.then_inc(s["relu_used"], 1)
                dve.wait_ge(s["relu_used"], n + 1)
            then(dve.tensor_tensor(isc, isc, see, ALU.mult))
            then(dve.tensor_scalar(add_a, see, -1.0, MASKED, ALU.add, ALU.mult))
            then(dve.tensor_tensor(isc, isc, add_a, ALU.add))
            for _ in range(TOPK // 8):
                for t in range(TT):
                    ins = dve.max(top8[:, 8 * t:8 * t + 8], isc[:, t, :])
                then(ins)
                for t in range(TT):
                    ins = dve.match_replace(isc[:, t, :], top8[:, 8 * t:8 * t + 8], isc[:, t, :], TAKEN)
                then(ins)
            then(dve.tensor_scalar(isc, isc, -2.0e38, None, ALU.is_le))
            then(dve.tensor_tensor(isc, isc, see, ALU.mult))
            dve.tensor_scalar(add_a, isc, -1.0, FAR, ALU.add, ALU.mult).then_inc(s["mask_ready"], 1)
            g0 = G["gate"]
            lo_of(g0, g0 + 1, g0 + 2)

            def units(first, count, mask, extra):
                def maxima(u):
                    dve.wait_ge(s["scores_done"], u + 1)
                    c = 2 * (u % 2)
                    if u >= first + 2:
                        dve.wait_ge(s["probT_done"], u - 1)
                    if mask is not None:
                        m = mask(u).unsqueeze(1).broadcast_to((P, 2, S))
                        ins = dve.tensor_tensor(prob[:, u % 2], ps[:, 2 + u % 2, :].rearrange("p (a b) -> p a b", a=2), m, ALU.add)
                        ins.then_inc(s["scores_used"], 1)
                        dve.wait_ge(s["scores_used"], u + 1)
                        src, scale = prob[:, u % 2], (BQ ** -0.5 if u < 8 else HD ** -0.5)
                    else:
                        n = P if (u - 16) % 2 == 0 else S
                        src, scale = ps[:, 2 + u % 2, 0:2 * n].rearrange("p (a b) -> p a b", a=2), 1.0
                    then(dve.tensor_reduce(rowmax[:, c:c + 2], src, AX_X, ALU.max))
                    dve.tensor_scalar(neg_max[:, c:c + 2], rowmax[:, c:c + 2], -scale, None, ALU.mult).then_inc(s["neg_ready"], 1)

                maxima(first)
                for u in range(first, first + count):
                    if u + 1 < first + count:
                        maxima(u + 1)
                    c = 2 * (u % 2)
                    dve.wait_ge(s["exp_done"], u + 1)
                    then(dve.reciprocal(row_inv[:, c:c + 2], row_sum[:, c:c + 2]))
                    for j in range(2):
                        if mask is not None:
                            p = prob[:, u % 2, j, :]
                        else:
                            p = probm[:, u % 2, j, 0:(P if (u - 16) % 2 == 0 else S)]
                        ins = dve.tensor_scalar(p, p, row_inv[:, c + j:c + j + 1], None, ALU.mult)
                    ins.then_inc(s["prob_ready"], 1)
                    extra(u)

            def gate_lo(u):
                if u % 2 == 1:
                    lo(g0 + 3 + u // 2)

            units(0, 16, lambda u: (add_b if u < 8 else add_a)[:, u % 2, :], gate_lo)
            for c in range(0, DC, 2):
                dve.wait_ge(s["ohi_ready"], c // 2 + 1)
                dve.tensor_tensor(x_lo[:, c:c + 2, :], o_T[:, c:c + 2, :], f32(x_hi[:, c:c + 2, :]), ALU.subtract).then_inc(s["olo_ready"], 1)
            b0 = G["branch"]
            lo_of(b0 + 3, b0 + 4, b0 + 5, b0 + 6)
            dve.wait_ge(s["gate_copied"], 4)
            for c in range(2):
                sl = slice(512 * c, 512 * c + 512)
                sl_b = slice(D + 512 * c, D + 512 * c + 512)
                dve.wait_ge(s["products_done"], b0 + c + 1)
                dve.tensor_tensor(xn[:, :, sl], ps[:, 2 * c:2 * c + 2, :], gates[:, :, sl], ALU.mult)
                dve.wait_ge(s["products_done"], b0 + 2 + c + 1)
                then(dve.tensor_tensor(gates[:, :, sl_b], ps[:, 4 + 2 * c:6 + 2 * c, :], gates[:, :, sl_b], ALU.mult))
                ins = dve.tensor_tensor(xn[:, :, sl], xn[:, :, sl], gates[:, :, sl_b], ALU.add)
                if c == 1:
                    ins.then_inc(s["xn_ready"], 1)
            operand_lo(1, None)
            lo_of(b0 + 7)
            f0 = G["ffn0"]
            lo_of(f0, f0 + 1, f0 + 2)
            add_residual([G["out"] + 1, G["out"] + 3])
            normalize(1)
            operand_lo(2, V_FFN1)

            def ffn(n0, f):
                def post(p, n_gate, i=None):
                    par = p % 2
                    P0 = PAIRS * f + p
                    more = 0 if i is None else 2 * i
                    done = 0 if i is None else 6 * i
                    if f == 0:
                        for ft in range(4):
                            col = 22 * (ft // 2) + 2 * p + ft % 2
                            first = 4 * p + ft + 1
                            both = 4 * p + 2 * (ft // 2) + 2
                            dve.wait_ge(s["conv_first"], both if i is None else 8 * i + both)
                            dst = conv[:, par, ft, :]
                            base = 256 * (ft % 2)
                            for tap in range(2):
                                back = 2 - tap
                                c = 44 * tap + col
                                w = vcol[:, 1, c:c + 1] if i is None else vcol[:, 1, bass.ds(i * 4 + c, 1)]
                                ins = dve.scalar_tensor_tensor(dst[:, back:S], ps[:, 2 * par + ft // 2, base:base + S - back], w,
                                                               dst[:, back:S], ALU.mult, ALU.add)
                                if tap == 0:
                                    ins.then_inc(s["conv_step"], 1)
                                    dve.wait_ge(s["conv_step"], first if i is None else 8 * i + first)
                        ins.then_inc(s["conv_done"], 1)
                        dve.wait_ge(s["gated"], more + P0 + 1)
                        dve.tensor_tensor(hid[:, par, :], act_g[:, par, :], conv[:, par, 2:4, :].rearrange("p a b -> p (a b)"),
                                          ALU.mult).then_inc(s["hid_ready"], 1)
                    else:
                        dve.wait_ge(s["products_done"], done + (n_gate + 2))
                        dve.wait_ge(s["gated"], more + P0 + 1)
                        dve.tensor_tensor(hid[:, par, :], act_g[:, par, :], ps[:, 2 * par + 1, :], ALU.mult).then_inc(s["hid_ready"], 1)

                def post_lo(p, i=None):
                    par = p % 2
                    first = 3 + PAIRS * f + p + 1
                    dve.wait_ge(s["hhi_ready"], first if i is None else 2 * i + first)
                    dve.tensor_tensor(hid_lo[:, 2 * par:2 * par + 2, :].rearrange("p a b -> p (a b)"), hid[:, par, :],
                                      f32(hid_hi[:, 2 * par:2 * par + 2, :].rearrange("p a b -> p (a b)")),
                                      ALU.subtract).then_inc(s["hlo_ready"], 1)

                lo(n0 + 3)
                post(0, n0)
                lo(n0 + 4)
                post_lo(0)
                lo(n0 + 5)
                post(1, n0 + 2)
                lo(n0 + 6)
                post_lo(1)
                lo(n0 + 7)
                with dve.Fori(0, 4) as i:
                    for q in range(2):
                        lo(n0 + 8 + 3 * q, i)
                        post(2 + q, n0 + 5 + 3 * q, i)
                        lo(n0 + 9 + 3 * q, i)
                        post_lo(2 + q, i)
                        lo(n0 + 10 + 3 * q, i)
                n1 = n0 + 29
                lo_next(n1 + 3)
                post(10, n1)
                lo_next(n1 + 4)
                post_lo(10)
                lo_next(n1 + 5)
                lo_next(n1 + 6)
                add_residual([n1 + 3, n1 + 3])

            def lo_next(n):
                if n < G["end"]:
                    lo(n)

            ffn(f0, 0)

            def final_norm(m, loads):
                variance(m)
                dve.wait_ge(s["rstd_ready"], m + 1)
                dve.wait_ge(s["final_in"], 16 * loads)
                for t in range(TT):
                    dve.scalar_tensor_tensor(h[:, t, :], h[:, t, :], rstd[:, 2 * m + t:2 * m + t + 1], g_final[:, :],
                                             ALU.mult, ALU.mult).then_inc(s["h_final"], 1)

            final_norm(2, 1)
            dve.wait_ge(s["h_final"], 2)
            lbl = [vcol[:, 0, V_LB + 8 * r:V_LB + 8 * r + 8] for r in range(2)]
            then(dve.tensor_tensor(lb, lbl[0], lbl[1], ALU.max))
            dve.tensor_tensor(lb_tmp[:, 0:8], lbl[0], lb, ALU.subtract)
            dve.tensor_tensor(lb_tmp[:, 8:16], lbl[1], lb, ALU.subtract).then_inc(s["lb_ready"], 1)
            normalize(3)
            dve.wait_ge(s["lb_ready"], 2)
            then(dve.tensor_tensor(lb_rest, lb_tmp[:, 0:8], lb_tmp[:, 8:16], ALU.add))
            then(dve.reciprocal(lb_rest, lb_rest))
            then(dve.tensor_tensor(lb, lb_tmp[:, 0:8], lb_rest, ALU.mult))
            then(dve.tensor_scalar(lb_rest, lb, -1.0, 1.0, ALU.mult, ALU.add))
            dve.memset(ones, 1.0)
            dve.memset(pairs.rearrange("p a b c -> p (a b c)"), 0.0)
            operand_lo(3, V_MIX2)
            nf = G["hf"]
            F = E[:, 0]
            for j in range(4):
                dve.wait_ge(s["f_sig"], j + 1)
                for hh in (2 * j, 2 * j + 1):
                    ins = dve.tensor_scalar(F[:, hh, :], K[:, hh, :], lb_rest[:, hh:hh + 1], lb[:, hh:hh + 1], ALU.mult, ALU.add)
                then(ins)
                lo(nf + 3 + j)
            dve.tensor_scalar(K.rearrange("p a b -> p (a b)"), F.rearrange("p a b -> p (a b)"), -1.0, 1.0, ALU.mult, ALU.add).then_inc(s["f_ready"], 1)
            for j in range(4):
                lo(nf + 7 + j)
            dve.wait_ge(s["logf_done"], 1)
            for hh in range(HEADS):
                for t in range(TT):
                    seg = CUM[:, hh, P * t:P * t + P]
                    ins = dve.tensor_tensor_scan(seg, ones, seg, 0.0, ALU.mult, ALU.add)
            ins.then_inc(s["cum_ready"], 1)
            dve.wait_ge(s["masks_in"], 16)

            def choose(level, count):
                for j in range(4):
                    dve.wait_ge(s["pairs_done"], 4 * count + j + 1)
                    dst = pairs[:, j // 2, 4 * (j % 2):4 * (j % 2) + 4, :]
                    m = masks[:, level, :].unsqueeze(1).broadcast_to((P, 4, P))
                    dve.copy_predicated(dst, m, ps[:, j, :].rearrange("p (a b) -> p a b", a=4)).then_inc(s["pairs_used"], 1)

            def decayed(lv):
                b = LEVELS[lv] if lv < len(LEVELS) else P
                dve.wait_ge(s["e_exp"], lv + 1)
                if lv >= 1:
                    dve.wait_ge(s["pairs_done"], 4 * lv + 4)
                flat = lambda v: v.rearrange("p h t -> p (h t)").rearrange("p (g w) -> p g w", w=2 * b)
                x, e, q, k = flat(X), flat(E[:, lv % 2]), flat(Q), flat(K)
                dve.tensor_tensor(x[:, :, b:2 * b], e[:, :, b:2 * b], q[:, :, b:2 * b], ALU.mult).then_inc(s["x_ready"], 1)
                dve.tensor_tensor(x[:, :, 0:b], e[:, :, 0:b], k[:, :, 0:b], ALU.mult).then_inc(s["x_ready"], 1)

            dve.wait_ge(s["q_ready"], 4)
            choose(len(LEVELS), 0)
            nh = nf + 8
            more = {0: (nh + 3,), 1: (nh + 4, nh + 5), 2: (nh + 6, nh + 7), 3: (nh + 8,), 4: (nh + 9, nh + 10)}
            for lv in range(len(LEVELS)):
                decayed(lv)
                lo_of(*more.get(lv, ()))
                choose(lv, lv + 1)
            decayed(len(LEVELS))
            variance(4)
            dve.wait_ge(s["rstd_ready"], 5)
            dve.wait_ge(s["og_copied"], 2)
            for t in range(TT):
                ins = dve.scalar_tensor_tensor(xn[:, t, :].rearrange("p (a b) -> p a b", a=2), ps[:, 2 * t:2 * t + 2, :],
                                               rstd[:, 8 + t:9 + t], ogate[:, t, :].rearrange("p (a b) -> p a b", a=2), ALU.mult, ALU.mult)
            ins.then_inc(s["xn_ready"], 1)
            operand_lo(4, V_OUT)
            no = G["hout"]
            for n in range(no + 3, no + 7):
                lo_next(n)
            add_residual([no + 1, no + 3])
            normalize(5)
            operand_lo(5, V_FFN2)
            ffn(G["ffn1"], 1)
            normalize(6)
            operand_lo(6, V_MIX2 + 8)
            nm = G["mq"]
            lo_of(*range(nm + 3, nm + 15))

            def output_lo(u):
                t, j = (u - 16) % 2, (u - 16) // 2
                dve.wait_ge(s["mo_hi"], u - 15)
                dst = slice(P * t, P * t + P)
                dve.tensor_tensor(x_lo[:, 2 * j:2 * j + 2, dst], ps[:, 4 + u % 2, 0:256].rearrange("p (a b) -> p a b", a=2),
                                  f32(x_hi[:, 2 * j:2 * j + 2, dst]), ALU.subtract).then_inc(s["mo_lo"], 1)

            units(16, 8, None, lambda u: output_lo(u - 1) if u > 16 else None)
            output_lo(23)
            no = G["mout"]
            lo_of(no + 3, no + 4, no + 5, no + 6)
            add_residual([no + 1, no + 3])
            normalize(7)
            operand_lo(7, V_FFN2 + 8)
            ffn(G["ffn2"], 2)
            final_norm(8, 2)

        @block.tensor
        def _(pe):
            parts = ((x_hi, w_hi), (x_hi, w_lo), (x_lo, w_hi))
            hid_parts = ((hid_hi, w_hi), (hid_hi, w_lo), (hid_lo, w_hi))

            def split_ready(n, i=None):
                pe.wait_ge(s["lo_ready"], (n + 1) if i is None else 6 * i + (n + 1))

            def token_product(n, chunks, bank, first, last, ops=parts, banks=None, i=None, ready=None):
                split_ready(n, i)
                _, _, _, kc, _, cols = granules[n]
                wide = (cols + 511) // 512
                for kk in range(kc):
                    if ready:
                        ready(chunks + kk)
                    for t in range(TT):
                        for c in range(wide):
                            w0 = kk * cols + 512 * c
                            n_c = min(512, cols - 512 * c)
                            for q, (x, w) in enumerate(ops):
                                ins = pe.matmul(ps[:, bank + 2 * c + t, 0:n_c], x[:, chunks + kk, P * t:P * t + P],
                                                w[:, n % RING, w0:w0 + n_c],
                                                start=(first and kk == 0 and q == 0), stop=(last and kk == kc - 1 and q == 2))
                ins.then_inc(s["products_done"], 1)

            def feature_product(n, bank, i=None, ready=None):
                split_ready(n, i)
                for f in range(2):
                    for k in range(DC):
                        if ready and f == 0:
                            ready(k)
                        for q, (x, w) in enumerate(parts):
                            ins = pe.matmul(ps[:, bank, S * f:S * f + S], w[:, n % RING, 256 * k + P * f:256 * k + P * f + P],
                                            x[:, k, :], start=(k == 0 and q == 0), stop=(k == DC - 1 and q == 2))
                ins.then_inc(s["products_done"], 1)

            def turn_xn(k):
                pe.wait_ge(s["xn_ready"], k + 1)
                for j in range(4):
                    for c in range(2):
                        for t in range(TT):
                            ins = pe.transpose(ps[:, j, 256 * c + P * t:256 * c + P * t + P],
                                               xn[:, t, P * (2 * j + c):P * (2 * j + c) + P], ident)
                    ins.then_inc(s["xt_done"], 1)

            def operand_ready(k):
                return lambda c: pe.wait_ge(s["xlo_ready"], DC * k + c + 1)

            pe.wait_ge(s["const_in"], 16)
            pe.wait_ge(s["small_in"], 16 * 12)
            for g, n in ((0, 75), (1, 88), (2, 88)):
                ins = pe.transpose(ps[:, 4, 88 * g:88 * g + n], vrow[0:n, g, :], ident[0:n, 0:n])
            ins.then_inc(s["vrow_T"], 1)
            pe.wait_ge(s["table_in"], 16)
            pe.wait_ge(s["setup"], 2)
            pe.matmul(ps[0:HEADS, 5, 0:BIAS_LEN], table[:, :], const[0:NBUCKET + 1, K_BUCKET:K_BUCKET + BIAS_LEN],
                      start=True, stop=True).then_inc(s["bias_ps"], 1)
            turn_xn(0)
            pe.wait_ge(s["bias_sb"], 1)
            for b in range(4):
                if b >= 2:
                    pe.wait_ge(s["proj_copied"], b - 1)
                bank = 4 + 2 * (b % 2)
                token_product(2 * b, 0, bank, True, False, ready=operand_ready(0) if b == 0 else None)
                token_product(2 * b + 1, 4, bank, False, True, ready=operand_ready(0) if b == 0 else None)

            groups = [0]

            def turn_group(pieces):
                n = groups[0]
                if n >= 2 and n != 7 and n != 8:
                    pe.wait_ge(s["group_copied"], n - 1 if n < 7 else n - 3)
                if n in (7, 8):
                    pe.wait_ge(s["hlo_ready"], 2 if n == 7 else 3)
                for i, piece in enumerate(pieces):
                    ins = pe.transpose(ps[0:piece.shape[1], n % 2, P * i:P * i + P], piece, ident)
                ins.then_inc(s["group_done"], 1)
                groups[0] += 1

            pe.wait_ge(s["idx_ready"], 1)
            turn_group([proj[:, t, C_IK:C_IK + HD] for t in range(TT)])
            for j in range(4):
                turn_group([proj[:, t, C_IQ + HD * hh:C_IQ + HD * hh + HD] for hh in (2 * j, 2 * j + 1) for t in range(TT)])
            pe.wait_ge(s["c_scaled"], 1)
            turn_group([proj[:, t, C_CQ + P * c:C_CQ + P * c + P] for c in range(2) for t in range(TT)])
            turn_group([proj[:, t, C_CKV:C_CKV + P] for t in range(TT)])
            pe.wait_ge(s["kr_ready"], 1)
            pe.wait_ge(s["qk_ready"], 1)
            turn_group([proj[:, t, C_G - BQ:C_G] for t in range(TT)])
            turn_group([proj[:, t, C_AK + HD * g:C_AK + HD * g + HD] for g in range(KV_HEADS) for t in range(TT)])
            for j in range(4):
                turn_group([proj[:, t, HD * hh:HD * hh + HD] for hh in (2 * j, 2 * j + 1) for t in range(TT)])
            for n in range(8):
                t, j = n // 4, n % 4
                if n >= 2:
                    pe.wait_ge(s["relu_done"], n - 1)
                for hh in range(2):
                    ins = pe.matmul(ps[:, 2 + n % 2, S * hh:S * hh + S], qi_T[:, 2 * j + hh, P * t:P * t + P], ki_T, start=True, stop=True)
                ins.then_inc(s["dots_done"], 1)
            n = G["uq"]
            split_ready(n)
            pe.wait_ge(s["proj_copied"], 4)
            for t in range(TT):
                for half in range(2):
                    for k in range(2):
                        for q, (x, w) in enumerate(hid_parts):
                            ins = pe.matmul(ps[:, 4 + 2 * t + half, 0:384], x[:, k, P * t:P * t + P],
                                            w[:, n % RING, 768 * k + 384 * half:768 * k + 384 * half + 384],
                                            start=(k == 0 and q == 0), stop=(k == 1 and q == 2))
            ins.then_inc(s["products_done"], 1)
            n = G["uk"]
            split_ready(n)
            pe.wait_ge(s["group_copied"], 11)
            for j in range(4):
                for q, (x, w) in enumerate(hid_parts):
                    ins = pe.matmul(ps[:, j // 2, S * (j % 2):S * (j % 2) + S], w[:, n % RING, P * j:P * j + P], x[:, 2, :],
                                    start=(q == 0), stop=(q == 2))
            ins.then_inc(s["products_done"], 1)
            n = G["uv"]
            split_ready(n)
            pe.wait_ge(s["relu_done"], 8)
            for t in range(TT):
                for q, (x, w) in enumerate(hid_parts):
                    ins = pe.matmul(ps[:, 2 + t, :], x[:, 2, P * t:P * t + P], w[:, n % RING, 0:512], start=(q == 0), stop=(q == 2))
            ins.then_inc(s["products_done"], 1)
            pe.wait_ge(s["qb_ready"], 1)
            pe.wait_ge(s["kv_copied"], 1)
            for j in range(4):
                turn_group([proj[:, t, C_QB + BQ * hh:C_QB + BQ * hh + BQ] for hh in (2 * j, 2 * j + 1) for t in range(TT)])
            pe.wait_ge(s["group_copied"], 15)

            def units(first, count, scores, values, sizes, extra):
                def score(u):
                    if u >= first + 2:
                        if u < 16:
                            pe.wait_ge(s["scores_used"], u - 1)
                        else:
                            pe.wait_ge(s["exp_done"], u - 1)
                    scores(u).then_inc(s["scores_done"], 1)

                score(first)
                for u in range(first, first + count):
                    if u + 1 < first + count:
                        score(u + 1)
                    extra(u)
                    pe.wait_ge(s["prob_ready"], u + 1)
                    if u >= first + 2:
                        pe.wait_ge(s["probT_copied"], u - 1)
                    buf, kt = sizes(u)
                    for j in range(2):
                        for k in range(kt):
                            ins = pe.transpose(ps[:, u % 2, P * (kt * j + k):P * (kt * j + k) + P], buf[:, u % 2, j, P * k:P * k + P], ident)
                    ins.then_inc(s["probT_done"], 1)
                    pe.wait_ge(s["probT_copied"], u + 1)
                    if u >= first + 2:
                        if u < 16:
                            pe.wait_ge(s["o_copied"], u - 1)
                        else:
                            pe.wait_ge(s["mo_lo"], u - 17)
                    values(u).then_inc(s["pv_done"], 1)

            def scores1(u):
                t, j = u % 2, (u % 8) // 2
                for hh in range(2):
                    head = 2 * j + hh
                    q, k = (qb_T, kb_T[:, head, :]) if u < 8 else (qa_T, ka_T[:, head // 4, :])
                    ins = pe.matmul(ps[:, 2 + u % 2, S * hh:S * hh + S], q[:, head, P * t:P * t + P], k, start=True, stop=True)
                return ins

            def values1(u):
                j = (u % 8) // 2
                for hh in range(2):
                    head = 2 * j + hh
                    for k in range(TT):
                        v = v_b[:, k, HD * head:HD * head + HD] if u < 8 else proj[:, k, C_AV + HD * (head // 4):C_AV + HD * (head // 4) + HD]
                        ins = pe.matmul(ps[HD * hh:HD * hh + HD, 4 + u % 2, 0:P], v, prob_T[:, u % 2, hh, k, :], start=(k == 0), stop=(k == TT - 1))
                return ins

            g0 = G["gate"]

            def gate_product(u):
                if u % 2 == 0:
                    r = u // 2
                    if r % 2 == 0 and r >= 2:
                        pe.wait_ge(s["gate_copied"], r // 2)
                    token_product(g0 + r, 4 * (r % 2), 6, r % 2 == 0, r % 2 == 1)

            units(0, 16, scores1, values1, lambda u: (prob, TT), gate_product)
            b0 = G["branch"]
            for c in range(4):
                if c % 2 == 0:
                    pe.wait_ge(s["o_copied"], 16)
                    pe.wait_ge(s["gate_copied"], 4)
                token_product(b0 + c, 4 * (c // 2), 4 * (c // 2) + 2 * (c % 2), True, True,
                              ready=(lambda k: pe.wait_ge(s["olo_ready"], k // 2 + 1)) if c % 2 == 0 else None)
            turn_xn(1)

            def out_product(n0, ready):
                for c in range(2):
                    for k in range(2):
                        token_product(n0 + 2 * c + k, 4 * k, 4 + 2 * c, k == 0, k == 1, ready=ready if c == 0 else None)

            out_product(G["out"], operand_ready(1))
            turn_xn(2)

            def ffn(n0, f, k_turn):
                def up(p, n, i=None, ready=None):
                    par = p % 2
                    P0 = PAIRS * f + p
                    more = 0 if i is None else 2 * i
                    if p >= 2:
                        pe.wait_ge(s["conv_done"] if f == 0 else s["hid_ready"], more + P0 - 1)
                    feature_product(n, 2 * par, i, ready)
                    feature_product(n + 1, 2 * par + 1, i)

                def down(p, n, i=None, last=False):
                    first = 3 + PAIRS * f + p + 1
                    pe.wait_ge(s["hlo_ready"], first if i is None else 2 * i + first)
                    token_product(n, 2 * (p % 2), 4, p == 0, last, hid_parts, i=i)

                for k in range(DC):
                    operand_ready(k_turn)(k)
                up(0, n0)
                up(1, n0 + 2)
                down(0, n0 + 4)
                with pe.Fori(0, 4) as i:
                    for q in range(2):
                        up(2 + q, n0 + 5 + 3 * q, i)
                        down(1 + q, n0 + 7 + 3 * q, i)
                up(10, n0 + 29)
                down(9, n0 + 31)
                down(10, n0 + 32, last=True)

            ffn(G["ffn0"], 0, 2)
            turn_xn(3)
            for k in range(DC):
                operand_ready(3)(k)
            nf = G["hf"]
            for j in range(8):
                feature_product(nf + j, j)

            def products(level, count):
                for j in range(4):
                    t = j // 2
                    if count == 0:
                        pe.wait_ge(s["f_sig"], 4)
                    else:
                        pe.wait_ge(s["pairs_used"], 4 * (count - 1) + j + 1)
                    for hh in range(4):
                        head = 4 * (j % 2) + hh
                        tok = slice(P * t, P * t + P)
                        k, q = (K, Q) if count == 0 else (X, X)
                        ins = pe.matmul(ps[:, j, P * hh:P * hh + P], k[:, head, tok], q[:, head, tok], start=True, stop=True)
                    ins.then_inc(s["pairs_done"], 1)

            pe.wait_ge(s["q_ready"], 4)
            pe.wait_ge(s["f_ready"], 1)
            products(None, 0)
            nh = nf + 8
            for lv in range(len(LEVELS)):
                if lv < 4:
                    bank = 4 + 2 * (lv % 2)
                    if lv >= 2:
                        pe.wait_ge(s["inp_copied"], lv - 1)
                    token_product(nh + 2 * lv, 0, bank, True, False)
                    token_product(nh + 2 * lv + 1, 4, bank, False, True)
                pe.wait_ge(s["x_ready"], 2 * (lv + 1))
                products(lv, lv + 1)
            pe.wait_ge(s["x_ready"], 2 * (len(LEVELS) + 1))
            pe.wait_ge(s["og_copied"], 2)
            for head in range(HEADS):
                ins = pe.matmul(ps[:, 4 + head // 4, P * (head % 4):P * (head % 4) + P], X[:, head, 0:P], X[:, head, P:S], start=True, stop=True)
            ins.then_inc(s["cross_done"], 1)
            pe.wait_ge(s["pairs_used"], 32)
            pe.wait_ge(s["inp_copied"], 2)
            pe.wait_ge(s["cross_copied"], 1)
            for t in range(TT):
                for head in range(HEADS):
                    dst = ps[:, 2 * t + head // 4, P * (head % 4):P * (head % 4) + P]
                    cols = slice(P * head, P * head + P)
                    ins = pe.matmul(dst, pairs[:, t, head, :], inp[:, t, cols], start=True, stop=(t == 0))
                    if t == 1:
                        ins = pe.matmul(dst, pairs_x[:, head, :], inp[:, 0, cols], start=False, stop=True)
            ins.then_inc(s["o_done"], 1)
            turn_xn(4)
            out_product(G["hout"], operand_ready(4))
            turn_xn(5)
            ffn(G["ffn1"], 1, 5)
            turn_xn(6)
            for k in range(DC):
                operand_ready(6)(k)
            nm = G["mq"]
            for j in range(8):
                if j >= 4:
                    pe.wait_ge(s["mqk_copied"], j - 3)
                feature_product(nm + j, j % 4)
            for b in range(2):
                token_product(nm + 8 + 2 * b, 0, 4 + 2 * b, True, False)
                token_product(nm + 9 + 2 * b, 4, 4 + 2 * b, False, True)
            pe.wait_ge(s["mqk_copied"], 8)
            pe.wait_ge(s["bias_in"], 16)
            pe.wait_ge(s["mv_copied"], 2)

            def scores2(u):
                t, j = (u - 16) % 2, (u - 16) // 2
                n = P if t == 0 else S
                for hh in range(2):
                    head = 2 * j + hh
                    dst = ps[:, 2 + u % 2, n * hh:n * hh + n]
                    pe.matmul(dst, qm_T[:, head, P * t:P * t + P], km_T[:, head, 0:n], start=True, stop=False)
                    ins = pe.matmul(dst, reverse, bias[:, head, S - n:S], start=False, stop=True)
                return ins

            def values2(u):
                t, j = (u - 16) % 2, (u - 16) // 2
                kt = 1 + t
                flat = probm_T[:, u % 2].rearrange("p a b c -> p (a b c)")
                for hh in range(2):
                    head = 2 * j + hh
                    for k in range(kt):
                        at = P * (kt * hh + k)
                        ins = pe.matmul(ps[:, 4 + u % 2, P * hh:P * hh + P], v_m[:, k, P * head:P * head + P],
                                        flat[:, at:at + P], start=(k == 0), stop=(k == kt - 1))
                return ins

            units(16, 8, scores2, values2, lambda u: (probm, 1 + (u - 16) % 2), lambda u: None)
            pe.wait_ge(s["mo_lo"], 8)
            out_product(G["mout"], None)
            turn_xn(7)
            ffn(G["ffn2"], 2, 7)


_INS = ["x", "positions", "norm_mix_g", "w_in", "idx_k_norm_g", "q_a_norm_g", "kv_a_norm_g", "w_uq", "w_uk", "w_uv",
        "w_branch_a", "w_branch_b", "w_out", "norm_ffn_g", "w_up", "conv_w", "conv_b", "w_down", "norm_final_g",
        "norm_mix_2", "norm_ffn_2", "hgrn_w_in_2", "hgrn_lb_logits_2", "hgrn_out_norm_2", "hgrn_w_out_2",
        "moba_w_in_2", "moba_w_out_2", "rel_bias_table_2", "ffn_w13_2", "ffn_w2_2", "final_norm_2"]


def kernel(**inputs):
    import concourse.bacc as _bacc
    from concourse import mybir as _mybir
    from concourse.bass_utils import run_bass_kernel_spmd as _run

    nc = _bacc.Bacc("TRN2", target_bir_lowering=False, num_devices=1)
    arrays, args = {}, {}
    const, pair_masks = shape_constants()
    given = {name: inputs[name] for name in _INS}
    given["const"], given["pair_masks"] = const, pair_masks
    for name, value in given.items():
        v = np.ascontiguousarray(value)
        arrays[f"in_{name}"] = v
        args[name] = nc.dram_tensor(f"in_{name}", v.shape, _mybir.dt.from_np(v.dtype), kind="ExternalInput").ap()
    out = nc.dram_tensor("out", (1, S, D), _mybir.dt.float32, kind="ExternalOutput").ap()
    build(nc, args, out)
    return _run(nc, [arrays], core_ids=[0]).results[0]["out"]
```

```python
from contextlib import ExitStack

import concourse.bass as bass
import numpy as np
from concourse import mybir

F32 = mybir.dt.float32
F32R = mybir.dt.float32r
I32 = mybir.dt.int32
ALU = mybir.AluOpType
ACT = mybir.ActivationFunctionType
AX_X = mybir.AxisListType.X

P = 128
S = 256
TT = S // P
D = 1024
DC = D // P
NF = 2816
PAIRS = NF // 256
HEADS = 8
KV_HEADS = 2
HD = 64
TOPK = min(256, S // 4)
BQ = 96
MOBA_SCALE = 128 ** -0.5
EPS = 1e-6
NBUCKET = 32
BIAS_LEN = 384

C_AQ, C_AK, C_AV, C_IQ, C_IK, C_IW, C_CQ, C_CKV, C_KR, C_G, C_END = (
    0, 512, 640, 768, 1280, 1344, 1352, 1608, 1736, 1768, 3816)
C_QB = 768

MASKED = 1.0e38
TAKEN = -3.0e38
FAR = 1.0e30

V_MIX1, V_FFN1, V_MIX2, V_FFN2, V_OUT, V_LB, V_CQ, V_CKV = 0, 8, 16, 32, 48, 56, 72, 74

K_ID, K_REV, K_BUCKET, K_FREQ, K_END = 0, 128, 256, 256 + BIAS_LEN, 256 + BIAS_LEN + 24
LEVELS = [64, 32, 16, 8, 4, 2, 1]


def shape_constants():
    c = np.zeros((P, K_END), np.float32)
    c[:, K_ID:K_ID + P] = np.eye(P)
    c[:, K_REV:K_REV + P] = np.eye(P)[::-1]
    dist = S - 1 - np.arange(BIAS_LEN)
    n = np.maximum(dist, 0)
    big = np.maximum(n, 16).astype(np.float32)
    large = 16 + (np.log(big / np.float32(16)) / np.float32(np.log(64)) * np.float32(16)).astype(np.int32)
    bucket = np.where(n < 16, n, np.minimum(large, 31))
    for j in range(BIAS_LEN):
        c[bucket[j] if dist[j] >= 0 else NBUCKET, K_BUCKET + j] = 1.0
    inv = [500000.0 ** (-2 * j / 16) for j in range(8)] + [500000.0 ** (-2 * j / 32) for j in range(16)]
    c[:, K_FREQ:K_END] = np.array(inv, np.float32)
    s, t = np.arange(P)[:, None], np.arange(P)[None, :]
    m = np.zeros((P, len(LEVELS) + 1, P), np.int32)
    for i, b in enumerate(LEVELS):
        m[:, i] = (s // (2 * b) == t // (2 * b)) & (s % (2 * b) < b) & (t % (2 * b) >= b)
    m[:, -1] = s == t
    return c, m


def plan_granules():
    g, at = [], {}

    def mark(name):
        at[name] = len(g)

    def token_blocks(name, layer, c0, c1):
        for c in range(c0, c1, 512):
            for k in (0, 4):
                g.append((name, layer, k, 4, c, min(512, c1 - c)))

    def feature_blocks(name, layer, c0, c1):
        for c in range(c0, c1, 256):
            g.append((name, layer, 0, DC, c, 256))

    def ffn(mark_name, up, down, layer):
        mark(mark_name)
        for p in range(PAIRS + 1):
            if p < PAIRS:
                g.append((up, layer, 0, DC, 256 * p, 256))
                g.append((up, layer, 0, DC, NF + 256 * p, 256))
            if p >= 1:
                g.append((down, layer, 2 * (p - 1), 2, 0, D))

    mark("in")
    token_blocks("w_in", 0, 0, C_G)
    mark("gate0")
    token_blocks("w_in", 0, C_G, C_G + 512)
    mark("uq")
    g.append(("w_uq", 0, 0, 2, 0, 768))
    mark("uk")
    g.append(("w_uk", 0, 0, 1, 0, 512))
    mark("uv")
    g.append(("w_uv", 0, 0, 1, 0, 512))
    mark("gate")
    token_blocks("w_in", 0, C_G + 512, C_END)
    mark("branch_b")
    for c in (0, 512):
        g.append(("w_branch_b", 0, 0, 4, c, 512))
    mark("branch_a")
    for c in (0, 512):
        g.append(("w_branch_a", 0, 0, 4, c, 512))
    mark("out")
    token_blocks("w_out", 0, 0, D)
    ffn("ffn0", "w_up", "w_down", 0)
    mark("hf")
    feature_blocks("hgrn_w_in_2", 0, 1024, 2048)
    mark("hq")
    feature_blocks("hgrn_w_in_2", 0, 0, 1024)
    mark("hi")
    token_blocks("hgrn_w_in_2", 0, 2048, 3072)
    mark("hg")
    token_blocks("hgrn_w_in_2", 0, 3072, 4096)
    mark("hout")
    token_blocks("hgrn_w_out_2", 0, 0, D)
    ffn("ffn1", "ffn_w13_2", "ffn_w2_2", 0)
    mark("mq")
    for what in ("q0", "k0", "v0", "q1", "k1", "q2", "k2", "v1", "q3", "k3"):
        i = int(what[1])
        if what[0] == "v":
            token_blocks("moba_w_in_2", 0, 2048 + 512 * i, 2560 + 512 * i)
        else:
            c = 256 * i + (1024 if what[0] == "k" else 0)
            feature_blocks("moba_w_in_2", 0, c, c + 256)
    mark("mout")
    for k in (0, 4):
        for c in (0, 512):
            g.append(("moba_w_out_2", 0, k, 4, c, 512))
    ffn("ffn2", "ffn_w13_2", "ffn_w2_2", 1)
    mark("end")
    return g, at


def build(nc, a, out):
    granules, G = plan_granules()
    RING = 3
    GW = 2048

    ahead2 = {17: (9,), 18: (10,), 19: (11,), 20: (12,), 21: (13, 14), 23: (15,)}

    with ExitStack() as ctx:
        def sb(name, shape, dt=F32):
            return ctx.enter_context(nc.sbuf_tensor(name, shape, dt))

        raw = sb("raw", [P, RING, GW])
        w_hi = sb("w_hi", [P, RING, GW], F32R)
        w_lo = sb("w_lo", [P, RING, GW], F32R)
        x_hi = sb("x_hi", [P, DC, S], F32R)
        x_lo = sb("x_lo", [P, DC, S], F32R)
        hid_hi = sb("hid_hi", [P, 4, S], F32R)
        hid_lo = sb("hid_lo", [P, 4, S], F32R)
        h = sb("h", [P, TT, D])
        xn = sb("xn", [P, TT, D])
        g_final = sb("g_final", [P, D])
        const = sb("const", [P, K_END])
        vcol = sb("vcol", [P, 3, 88])
        stat = sb("stat", [P, 160])
        work = sb("work", [P, 21760])
        ps = ctx.enter_context(nc.psum_tensor("ps", [P, 8, 512], F32))
        bias_scratch = nc.dram_tensor("bias_scratch", (HEADS, BIAS_LEN), F32, kind="Internal").ap()

        ident = const[:, K_ID:K_ID + P]
        reverse = const[:, K_REV:K_REV + P]

        def region(start, *dims, parts=P):
            n = int(np.prod(dims))
            v = work[0:parts, start:start + n]
            names = "abcd"[:len(dims)]
            if len(dims) > 1:
                v = v.rearrange(f"p ({' '.join(names)}) -> p {' '.join(names)}", **dict(zip(names[1:], dims[1:])))
            return v

        proj = region(0, TT, C_G)
        gates = region(3536, TT, 2048)
        qi_T = region(7632, HEADS, S, parts=HD)
        qb_T = region(7632, HEADS, S, parts=BQ)
        qa_T = region(9680, HEADS, S, parts=HD)
        kb_T = region(11728, HEADS, S, parts=BQ)
        o_T = region(13776, 4, S)
        y_b = region(7632, TT, D)
        ka_T = region(15824, KV_HEADS, S, parts=HD)
        ki_T = region(16336, S, parts=HD)
        v_b = region(16592, TT, 512)
        prob = region(17616, 2, 2, S)
        prob_T = region(18640, 2, 2, TT, P)
        see = region(19664, TT, S)
        add_b = region(20176, TT, S)
        add_a = region(20688, TT, S)
        isc = region(21200, TT, S)
        vrow = region(9680, 3, P)
        posrow_i = region(11728, S).bitcast(I32)
        posrow = region(12240, S)
        pool_tmp = region(13776, 4, 160 * TT)
        g_ik = region(16592, HD)
        bias_row = region(17616, BIAS_LEN, parts=HEADS)

        conv = region(0, 2, 4, S)
        act_g = region(2048, 2, 512)
        hid = region(3072, 2, 512)

        Q = region(0, HEADS, S)
        K = region(2048, HEADS, S)
        CUM = region(4096, HEADS, S)
        E = region(6144, 2, HEADS, S)
        inp = region(10240, TT, D)
        ogate = region(12288, TT, D)
        pairs = region(14336, TT, HEADS, P)
        pairs_x = region(16384, HEADS, P)
        ones = region(19456, P)
        masks = region(19584, len(LEVELS) + 1, P).bitcast(I32)

        qm_T = region(0, HEADS, S)
        km_T = region(2048, HEADS, S)
        v_m = region(4096, TT, D)
        bias = region(6144, HEADS, S)
        probm = region(8192, 2, 2, S)
        probm_T = region(9216, 2, 2, TT, P)

        ssq = stat[:, 0:18]
        var = stat[:, 18:36]
        rstd = stat[:, 36:54]
        ssq6, var6, rstd6 = stat[:, 54:60], stat[:, 60:66], stat[:, 66:72]
        w_idx = stat[:, 72:88]
        top8 = stat[:, 88:104]
        rowmax = stat[:, 104:108]
        neg_max = stat[:, 108:112]
        row_sum = stat[:, 112:116]
        row_inv = stat[:, 116:120]
        lb = stat[:, 120:128]
        lb_rest = stat[:, 128:136]
        lb_tmp = stat[:, 136:152]
        minus_half = stat[:, 152:158]
        pos_col = stat[:, 158:160]
        trig = sb("trig", [P, 2, TT, 24])
        ang = sb("ang", [P, 4, TT * 24])
        pos_i = sb("pos_i", [P, TT], I32)
        table = sb("table", [NBUCKET + 1, HEADS])

        names = """small_in pos_in const_in gain_in table_in masks_in final_in final2_in bias_out bias_in out_done
            setup vrow_T vcol_done bias_ps bias_sb trig_ready
            hi_ready lo_ready products_done
            ssq_ready var_ready rstd_ready xn_ready xt_done xhi_ready xlo_ready h_added h_final
            proj_copied gate_copied ssq6_ready var6_ready rstd6_ready c_scaled idx_ready qk_ready kr_ready
            group_done group_copied dots_done relu_done relu_used qb_copied qb_ready kv_copied
            scores_done scores_used neg_ready exp_done prob_ready probT_done probT_copied pv_done o_copied
            ohi_ready olo_ready
            conv_first conv_step conv_done mo_lo ob_lo part_done yb_copied gate_sig b_gated gated hid_ready hhi_ready hlo_ready
            f_sig f_ready logf_done cum_ready q_ready e_ready e_exp x_ready pairs_done pairs_used
            cross_done cross_copied inp_copied og_copied o_done lb_ready
            mqk_copied mv_copied mo_hi dve_step act_step pool_step""".split()
        s = {n: ctx.enter_context(nc.semaphore(n)) for n in names}
        raw_in = [ctx.enter_context(nc.semaphore(f"raw_in{i}")) for i in range(RING)]
        x_in = [ctx.enter_context(nc.semaphore(f"x_in{i}")) for i in range(TT)]
        block = ctx.enter_context(nc.Block())

        def granule_views(n):
            name, layer, k0, kc, c0, cols = granules[n]
            dst = raw[:, n % RING, 0:kc * cols].rearrange("p (c n) -> p c n", c=kc)
            return dst, cols

        def turn_bank(k):
            return 4 if k in (2, 3, 4, 5, 7) else 0

        def f32(ap):
            return ap.bitcast(F32)

        class Chain:

            def __init__(self, eng, sem):
                self.eng, self.sem, self.n = eng, sem, 0

            def __call__(self, ins):
                self.n += 1
                ins.then_inc(self.sem, 1)
                self.eng.wait_ge(self.sem, self.n)

        @block.sync
        def _(sp):
            def load(n, i=None, step=None):
                name, layer, k0, kc, c0, cols = granules[n]
                more = 0 if i is None else 6 * i
                w = a[name][layer]
                if name in ("w_uq", "w_uk", "w_uv"):
                    w = w.rearrange("r h d -> r (h d)")
                if i is None:
                    src = w[k0 * P:(k0 + kc) * P, c0:c0 + cols]
                elif step == "columns":
                    src = w[k0 * P:(k0 + kc) * P, bass.ds(sp.snap(i * 512 + c0), cols)]
                else:
                    src = w[bass.ds(sp.snap(i * 512 + k0 * P), kc * P), c0:c0 + cols]
                dst, _ = granule_views(n)
                src = src.rearrange("(c p) n -> p c n", p=P)
                if n >= RING:
                    sp.wait_ge(s["lo_ready"], more + (n - RING + 1))
                sp.dma_start(dst, src).then_inc(raw_in[n % RING], 16)

            def load_ffn(n0):
                for n in range(n0, n0 + 5):
                    load(n)
                with sp.Fori(0, 4) as i:
                    for j in range(6):
                        load(n0 + 5 + j, i, "columns" if j % 3 < 2 else "rows")
                for n in range(n0 + 29, n0 + 33):
                    load(n)

            for t in range(TT):
                sp.dma_start(h[:, t, :], a["x"][0, P * t:P * t + P, :]).then_inc(x_in[t], 16)
            for n in range(G["ffn0"]):
                load(n)
            load_ffn(G["ffn0"])
            for n in range(G["hf"], G["ffn1"]):
                load(n)
            load_ffn(G["ffn1"])
            for n in range(G["mq"], G["ffn2"]):
                load(n)
            load_ffn(G["ffn2"])
            sp.wait_ge(s["h_final"], 4)
            sp.dma_start(out[0].rearrange("(t p) d -> p t d", p=P), h[:, :, :]).then_inc(s["out_done"], 16)
            sp.wait_ge(s["out_done"], 16)

        @block.gpsimd
        def _(pool):
            then = Chain(pool, s["pool_step"])

            def power(src, dst, ready, n, signal):
                w = src.shape[1]
                pool.wait_ge(ready, n)
                pool.tensor_tensor(dst, src, minus_half[:, 0:w], ALU.pow).then_inc(signal, 1)

            pool.dma_start(const[:, :], a["const"]).then_inc(s["const_in"], 16)
            pool.dma_start(pos_i[:, :], a["positions"][0].rearrange("(t p) -> p t", p=P), allow_slow_non_contiguous=True).then_inc(s["pos_in"], 16)
            pool.dma_start(posrow_i, a["positions"][0].partition_broadcast(P)).then_inc(s["pos_in"], 16)

            pool.dma_start(g_ik, a["idx_k_norm_g"][0].partition_broadcast(P)).then_inc(s["gain_in"], 16)
            pool.dma_start(table[0:NBUCKET, :], a["rel_bias_table_2"]).then_inc(s["table_in"], 16)
            pool.dma_start(g_final[:, :], a["norm_final_g"].partition_broadcast(P)).then_inc(s["final_in"], 16)

            pool.wait_ge(s["setup"], 2)
            def inverse_rms(m):
                for t in range(TT):
                    c = 2 * m + t
                    power(var[:, c:c + 1], rstd[:, c:c + 1], s["var_ready"], c + 1, s["rstd_ready"])

            inverse_rms(0)
            power(var6, rstd6, s["var6_ready"], 1, s["rstd6_ready"])
            pool.wait_ge(s["trig_ready"], 1)
            pool.wait_ge(s["proj_copied"], 4)

            def rotate(x, heads, width, off, half, freq):
                v = x.rearrange("p t (h w) -> p t h w", w=width)
                x1, x2 = v[:, :, :, off:off + half], v[:, :, :, off + half:off + 2 * half]
                n = TT * heads * half
                t = [pool_tmp[:, i, 0:n].rearrange("p (t h w) -> p t h w", t=TT, w=half) for i in range(4)]
                cos = trig[:, 0, :, freq:freq + half].unsqueeze(2).broadcast_to((P, TT, heads, half))
                sin = trig[:, 1, :, freq:freq + half].unsqueeze(2).broadcast_to((P, TT, heads, half))
                pool.tensor_tensor(t[0], x1, cos, ALU.mult)
                pool.tensor_tensor(t[1], x2, sin, ALU.mult)
                pool.tensor_tensor(t[2], x1, sin, ALU.mult)
                then(pool.tensor_tensor(t[3], x2, cos, ALU.mult))
                pool.tensor_tensor(x1, t[0], t[1], ALU.subtract)
                return pool.tensor_tensor(x2, t[2], t[3], ALU.add)

            rotate(proj[:, :, C_AQ:C_AV], 10, HD, 0, 8, 0).then_inc(s["qk_ready"], 1)
            pool.wait_ge(s["qk_ready"], 1)
            rotate(proj[:, :, C_KR:C_G], 1, 32, 0, 16, 8).then_inc(s["kr_ready"], 1)

            def lo_pool(first, count):
                pool.wait_ge(s["lo_ready"], first)
                for n in range(first, first + count):
                    _, _, _, kc, _, cols = granules[n]
                    sl = slice(0, kc * cols)
                    pool.wait_ge(s["hi_ready"], n + 1)
                    pool.tensor_tensor(w_lo[:, n % RING, sl], raw[:, n % RING, sl], f32(w_hi[:, n % RING, sl]), ALU.subtract).then_inc(s["lo_ready"], 1)

            g0 = G["gate"]
            lo_pool(g0 + 1, 9)
            pool.wait_ge(s["yb_copied"], 2)
            pool.wait_ge(s["gate_sig"], 4)
            pool.tensor_tensor(gates[:, :, D:2 * D], y_b, gates[:, :, D:2 * D], ALU.mult).then_inc(s["b_gated"], 1)
            lo_pool(g0 + 10, 2)
            for m in range(1, 4):
                inverse_rms(m)
            pool.wait_ge(s["cum_ready"], 1)
            cum = CUM.rearrange("p h t -> p (h t)")
            for lv, b in enumerate(LEVELS):
                if lv >= 2:
                    pool.wait_ge(s["pairs_done"], 4 * lv)
                c = cum.rearrange("p (g w) -> p g w", w=2 * b)
                e = E[:, lv % 2].rearrange("p h t -> p (h t)").rearrange("p (g w) -> p g w", w=2 * b)
                mid = c[:, :, b - 1:b].broadcast_to((P, HEADS * S // (2 * b), b))
                pool.tensor_tensor(e[:, :, b:2 * b], c[:, :, b:2 * b], mid, ALU.subtract)
                pool.tensor_tensor(e[:, :, 0:b], mid, c[:, :, 0:b], ALU.subtract).then_inc(s["e_ready"], 1)
            pool.wait_ge(s["pairs_done"], 4 * len(LEVELS))
            e = E[:, len(LEVELS) % 2]
            pool.tensor_tensor(e[:, :, 0:P], CUM[:, :, P - 1:P].broadcast_to((P, HEADS, P)), CUM[:, :, 0:P],
                               ALU.subtract).then_inc(s["e_ready"], 1)
            for m in range(4, 7):
                inverse_rms(m)
            lo_pool(G["mq"] + 9, 7)
            for m in range(7, 9):
                inverse_rms(m)

        @block.scalar
        def _(act):
            then = Chain(act, s["act_step"])

            def hi(n, i=None):
                more, turns = (0, 0) if i is None else (6 * i, 32 * i)
                _, _, _, kc, _, cols = granules[n]
                act.wait_ge(raw_in[n % RING], turns + 16 * (n // RING + 1))
                if n >= RING:
                    act.wait_ge(s["products_done"], more + (n - RING + 1))
                act.activation(w_hi[:, n % RING, 0:kc * cols], raw[:, n % RING, 0:kc * cols], ACT.Copy).then_inc(s["hi_ready"], 1)

            def hi_of(*ns):
                for n in ns:
                    hi(n)

            def operand_hi(k, gain):
                for c in range(DC):
                    if c % 2 == 0:
                        act.wait_ge(s["xt_done"], 4 * k + c // 2 + 1)
                    act.activation(x_hi[:, c, :], ps[:, turn_bank(k) + c // 2, 256 * (c % 2):256 * (c % 2) + 256], ACT.Copy,
                                   scale=1.0 if gain is None else vcol[:, 0, gain + c:gain + c + 1]).then_inc(s["xhi_ready"], 1)

            def squares(m, sem, before):
                for t in range(TT):
                    act.wait_ge(sem, before + t + 1)
                    act.activation(xn[:, t, :], h[:, t, :], ACT.Square,
                                   accum_out=ssq[:, 2 * m + t:2 * m + t + 1]).then_inc(s["ssq_ready"], 1)

            def units(first, count, scale, psum_scores, copy_o, extra):
                def exps(u):
                    act.wait_ge(s["neg_ready"], u + 1)
                    for j in range(2):
                        src, dst = psum_scores(u, j)
                        ins = act.activation(dst, src, ACT.Exp, scale=scale(u),
                                             bias=neg_max[:, 2 * (u % 2) + j:2 * (u % 2) + j + 1],
                                             accum_out=row_sum[:, 2 * (u % 2) + j:2 * (u % 2) + j + 1])
                    ins.then_inc(s["exp_done"], 1)

                def output(u):
                    act.wait_ge(s["pv_done"], u + 1)
                    copy_o(u)

                if first == 0:
                    exps(first)
                for u in range(first, first + count):
                    if u + 1 < first + count:
                        exps(u + 1)
                    if u > first:
                        output(u - 1)
                    act.wait_ge(s["probT_done"], u + 1)
                    n, dst = prob_T_of(u)
                    act.activation(dst, ps[:, u % 2, 0:n], ACT.Copy).then_inc(s["probT_copied"], 1)
                    extra(u)
                output(first + count - 1)

            def prob_T_of(u):
                if u < 16:
                    return 512, prob_T[:, u % 2].rearrange("p a b c -> p (a b c)")
                n = 256 if (u - 16) % 2 == 0 else 512
                return n, probm_T[:, u % 2].rearrange("p a b c -> p (a b c)")[:, 0:n]

            for r, name in ((V_MIX1, "norm_mix_g"), (V_FFN1, "norm_ffn_g"), (V_MIX2, "norm_mix_2"), (V_FFN2, "norm_ffn_2"),
                            (V_OUT, "hgrn_out_norm_2"), (V_LB, "hgrn_lb_logits_2"), (V_CQ, "q_a_norm_g"), (V_CKV, "kv_a_norm_g")):
                v = a[name]
                v = v.rearrange("l (c p) -> (l c) p", p=P)
                act.dma_start(vrow[r:r + v.shape[0], 0, :], v).then_inc(s["small_in"], 16)
            taps = a["conv_w"][0].rearrange("j (c p) -> j c p", p=P)
            for j in range(3):
                act.dma_start(vrow[44 * (j % 2):44 * (j % 2) + 44, 1 + j // 2, :], taps[j]).then_inc(s["small_in"], 16)
            act.dma_start(vrow[44:88, 2, :], a["conv_b"][0].rearrange("(c p) -> c p", p=P)).then_inc(s["small_in"], 16)
            for t in range(TT):
                act.wait_ge(x_in[t], 16)
                act.activation(xn[:, t, :], h[:, t, :], ACT.Square, accum_out=ssq[:, t:t + 1]).then_inc(s["ssq_ready"], 1)
            hi(0)
            act.wait_ge(s["vrow_T"], 1)
            act.activation(vcol[:, 0, 0:75], ps[:, 4, 0:75], ACT.Copy)
            act.activation(vcol[:, 1:3, :].rearrange("p g n -> p (g n)"), ps[:, 4, 88:264], ACT.Copy).then_inc(s["vcol_done"], 1)
            act.wait_ge(s["bias_ps"], 1)
            act.activation(bias_row[:, :], ps[0:HEADS, 5, 0:BIAS_LEN], ACT.Copy).then_inc(s["bias_sb"], 1)
            act.wait_ge(s["bias_sb"], 1)
            act.dma_start(bias_scratch, bias_row[:, :]).then_inc(s["bias_out"], 16)
            act.wait_ge(s["vcol_done"], 1)
            operand_hi(0, V_MIX1)
            hi_of(1, 2)

            def copy_proj(b):
                c0, c1 = 512 * b, min(512 * b + 512, C_G)
                act.wait_ge(s["products_done"], 2 * b + 2)
                bank = 4 + 2 * (b % 2)
                act.activation(proj[:, :, c0:c1], ps[:, bank:bank + 2, 0:c1 - c0], ACT.Copy).then_inc(s["proj_copied"], 1)

            hi_of(3, 4)
            copy_proj(0)
            act.wait_ge(s["setup"], 3)
            act.activation(trig[:, 1].rearrange("p t f -> p (t f)"), ang[:, 0, :], ACT.Sin)
            act.activation(trig[:, 0].rearrange("p t f -> p (t f)"), ang[:, 1, :], ACT.Sin).then_inc(s["trig_ready"], 1)
            hi_of(5, 6)
            copy_proj(1)
            hi_of(7, 8)
            copy_proj(2)
            hi_of(9)
            copy_proj(3)
            act.wait_ge(s["proj_copied"], 4)
            for i, (c0, n) in enumerate(((C_IK, HD), (C_CQ, 256), (C_CKV, P))):
                for t in range(TT):
                    ins = act.activation(xn[:, t, 256 * i:256 * i + n], proj[:, t, c0:c0 + n], ACT.Square, accum_out=ssq6[:, 2 * i + t:2 * i + t + 1])
            ins.then_inc(s["ssq6_ready"], 1)
            hi_of(10)
            act.wait_ge(s["rstd6_ready"], 1)
            for i, (c0, n) in ((1, (C_CQ, 256)), (2, (C_CKV, P))):
                for t in range(TT):
                    ins = act.activation(proj[:, t, c0:c0 + n], proj[:, t, c0:c0 + n], ACT.Copy, scale=rstd6[:, 2 * i + t:2 * i + t + 1])
            ins.then_inc(s["c_scaled"], 1)
            hi_of(11, 12)

            def copy_gate(b, last, bank):
                act.wait_ge(s["products_done"], last + 1)
                act.activation(gates[:, :, 512 * b:512 * b + 512], ps[:, bank:bank + 2, :], ACT.Copy).then_inc(s["gate_copied"], 1)

            copy_gate(0, G["gate0"] + 1, 4)

            def group(n, dst, src, last=True, **kw):
                act.wait_ge(s["group_done"], n + 1)
                ins = act.activation(dst, src, ACT.Copy, **kw)
                if last:
                    ins.then_inc(s["group_copied"], 1)

            group(0, ki_T, ps[0:HD, 0, 0:S])
            for j in range(4):
                group(1 + j, qi_T[:, 2 * j:2 * j + 2, :].rearrange("p a b -> p (a b)"), ps[0:HD, (1 + j) % 2, :])

            def relus(t):
                for j in range(4):
                    n = 4 * t + j
                    act.wait_ge(s["dots_done"], n + 1)
                    if n >= 2:
                        act.wait_ge(s["relu_used"], n - 1)
                    act.activation(prob[:, n % 2].rearrange("p a b -> p (a b)"), ps[:, 2 + n % 2, :], ACT.Relu,
                                   scale=HD ** -0.5).then_inc(s["relu_done"], 1)

            for c in range(3):
                act.wait_ge(s["group_done"], 6 + c // 2)
                act.activation(hid_hi[:, c, :], ps[:, (5 + c // 2) % 2, 256 * (c % 2):256 * (c % 2) + 256], ACT.Copy,
                               scale=vcol[:, 0, V_CQ + c:V_CQ + c + 1]).then_inc(s["hhi_ready"], 1)
            group(7, kb_T[HD:BQ, :, :], ps[HD:BQ, 1, 0:S].unsqueeze(1).broadcast_to((BQ - HD, HEADS, S)))
            group(8, ka_T.rearrange("p a b -> p (a b)"), ps[0:HD, 0, :])
            for j in range(4):
                group(9 + j, qa_T[:, 2 * j:2 * j + 2, :].rearrange("p a b -> p (a b)"), ps[0:HD, (9 + j) % 2, :])
            act.wait_ge(s["bias_out"], 16)
            relus(0)
            relus(1)
            act.wait_ge(s["products_done"], G["uq"] + 1)
            act.activation(proj[:, 0, C_QB:C_QB + 768].rearrange("p (a b) -> p a b", a=2), ps[:, 4:6, 0:384], ACT.Copy)
            act.activation(proj[:, 1, C_QB:C_QB + 768].rearrange("p (a b) -> p a b", a=2), ps[:, 6:8, 0:384], ACT.Copy).then_inc(s["qb_copied"], 1)
            act.wait_ge(s["products_done"], G["uv"] + 1)
            for bank in range(2):
                src = ps[:, bank, :].rearrange("p (a b) -> p a b", a=2)
                act.activation(kb_T[0:HD, 4 * bank:4 * bank + 3:2, :], src[0:HD], ACT.Copy)
                act.activation(kb_T[0:HD, 4 * bank + 1:4 * bank + 4:2, :], src[HD:P], ACT.Copy)
            act.activation(v_b, ps[:, 2:4, :], ACT.Copy).then_inc(s["kv_copied"], 1)
            g0 = G["gate"]
            hi(g0)
            for j in range(4):
                group(13 + j, qb_T[:, 2 * j:2 * j + 2, :].rearrange("p a b -> p (a b)"), ps[0:BQ, (13 + j) % 2, :])
            def scores1(u, j):
                return prob[:, u % 2, j, :], prob[:, u % 2, j, :]

            def copy_o1(u):
                t, j = u % 2, (u % 8) // 2
                dst = (hid_hi if u < 8 else o_T)[:, j, P * t:P * t + P]
                act.activation(dst, ps[:, 4 + u % 2, 0:P], ACT.Copy).then_inc(s["o_copied"], 1)

            bb, ba = G["branch_b"], G["branch_a"]

            def copy_yb(c):
                act.wait_ge(s["products_done"], bb + c + 1)
                act.activation(y_b[:, :, 512 * c:512 * c + 512], ps[:, 6:8, :], ACT.Copy).then_inc(s["yb_copied"], 1)

            def fill_work(u):
                if u < 2:
                    hi(g0 + 1 + u)
                elif u % 2 == 0:
                    hi(g0 + 2 + u // 2)
                if u in (3, 7, 11):
                    copy_gate(1 + u // 4, g0 + 2 * (u // 4) + 1, 6)
                if u == 13:
                    copy_yb(0)

            units(0, 16, lambda u: (BQ ** -0.5 if u < 8 else HD ** -0.5), scores1, copy_o1, fill_work)
            for c in range(0, 4, 2):
                if c == 0:
                    act.wait_ge(s["o_copied"], 16)
                act.activation(x_hi[:, c:c + 2, :], o_T[:, c:c + 2, :], ACT.Copy).then_inc(s["ohi_ready"], 1)
            copy_yb(1)
            for b in range(4):
                act.activation(gates[:, :, 512 * b:512 * b + 512], gates[:, :, 512 * b:512 * b + 512],
                               ACT.Sigmoid).then_inc(s["gate_sig"], 1)
            hi_of(ba + 2, ba + 3, ba + 4)
            operand_hi(1, None)
            hi_of(ba + 5)
            f0 = G["ffn0"]
            hi_of(f0, f0 + 1)
            squares(1, s["h_added"], 0)
            hi_of(f0 + 2)
            operand_hi(2, V_FFN1)

            def ffn(n0, f):
                def post(p, n_gate, i=None):
                    par = p % 2
                    more = 0 if i is None else 2 * i
                    done = 0 if i is None else 6 * i
                    P0 = PAIRS * f + p
                    if f == 0:
                        act.wait_ge(s["products_done"], done + (n_gate + 1))
                        for ft in range(4):
                            if ft == 2:
                                act.wait_ge(s["products_done"], done + (n_gate + 2))
                            col = 22 * (ft // 2) + 2 * p + ft % 2
                            c = col if i is None else i * 4 + col
                            last = vcol[:, 2, c:c + 1] if i is None else vcol[:, 2, bass.ds(c, 1)]
                            bias_c = vcol[:, 2, 44 + c:45 + c] if i is None else vcol[:, 2, bass.ds(c + 44, 1)]
                            act.activation(conv[:, par, ft, :], ps[:, 2 * par + ft // 2, 256 * (ft % 2):256 * (ft % 2) + 256],
                                           ACT.Identity, scale=last, bias=bias_c).then_inc(s["conv_first"], 1)
                        act.wait_ge(s["conv_done"], more + P0 + 1)
                        act.activation(act_g[:, par, :], conv[:, par, 0:2, :].rearrange("p a b -> p (a b)"), ACT.Silu).then_inc(s["gated"], 1)
                    else:
                        act.wait_ge(s["products_done"], done + (n_gate + 1))
                        act.activation(act_g[:, par, :], ps[:, 2 * par, :], ACT.Silu).then_inc(s["gated"], 1)

                def post_hi(p, i=None):
                    par = p % 2
                    P0 = PAIRS * f + p
                    more = 0 if i is None else 2 * i
                    act.wait_ge(s["hid_ready"], more + P0 + 1)
                    act.activation(hid_hi[:, 2 * par:2 * par + 2, :].rearrange("p a b -> p (a b)"), hid[:, par, :],
                                   ACT.Copy).then_inc(s["hhi_ready"], 1)

                hi(n0 + 3)
                post(0, n0)
                hi(n0 + 4)
                post_hi(0)
                hi(n0 + 5)
                post(1, n0 + 2)
                hi(n0 + 6)
                post_hi(1)
                hi(n0 + 7)
                with act.Fori(0, 4) as i:
                    for q in range(2):
                        hi(n0 + 8 + 3 * q, i)
                        post(2 + q, n0 + 5 + 3 * q, i)
                        hi(n0 + 9 + 3 * q, i)
                        post_hi(2 + q, i)
                        hi(n0 + 10 + 3 * q, i)
                n1 = n0 + 29
                hi_next(n1 + 3)
                post(10, n1)
                hi_next(n1 + 4)
                post_hi(10)
                hi_next(n1 + 5)

            def hi_next(n):
                if n < G["end"]:
                    hi(n)

            ffn(f0, 0)
            squares(2, s["h_added"], 2)
            squares(3, s["h_final"], 0)
            hi(G["hf"] + 2)
            act.dma_start(g_final[:, :], a["final_norm_2"].partition_broadcast(P)).then_inc(s["final2_in"], 16)
            act.dma_start(masks, a["pair_masks"]).then_inc(s["masks_in"], 16)
            operand_hi(3, V_MIX2)
            act.wait_ge(s["lb_ready"], 1)
            act.activation(lb_tmp, lb_tmp, ACT.Exp).then_inc(s["lb_ready"], 1)
            nf = G["hf"]

            for j in range(4):
                act.wait_ge(s["products_done"], nf + j + 1)
                act.activation(K[:, 2 * j:2 * j + 2, :].rearrange("p a b -> p (a b)"), ps[:, j, :], ACT.Sigmoid).then_inc(s["f_sig"], 1)
                hi(nf + 3 + j)
            for j in range(4):
                act.wait_ge(s["products_done"], nf + 5 + j)
                act.activation(Q[:, 2 * j:2 * j + 2, :].rearrange("p a b -> p (a b)"), ps[:, 4 + j, :], ACT.Silu).then_inc(s["q_ready"], 1)
                hi(nf + 7 + j)
            act.wait_ge(s["f_ready"], 1)
            act.activation(CUM.rearrange("p a b -> p (a b)"), E[:, 0].rearrange("p a b -> p (a b)"), ACT.Ln).then_inc(s["logf_done"], 1)

            def exp_level(lv):
                act.wait_ge(s["e_ready"], lv + 1)
                if lv < len(LEVELS):
                    e = E[:, lv % 2].rearrange("p a b -> p (a b)")
                    act.activation(e, e, ACT.Exp).then_inc(s["e_exp"], 1)
                else:
                    e = E[:, lv % 2]
                    act.activation(e[:, :, P:S], CUM[:, :, P:S], ACT.Exp)
                    act.activation(e[:, :, 0:P], e[:, :, 0:P], ACT.Exp).then_inc(s["e_exp"], 1)

            def copy_block(b):
                bank = 4 + 2 * (b % 2)
                act.wait_ge(s["products_done"], nf + 8 + 2 * b + 2)
                c = 512 * (b % 2)
                dst = (inp if b < 2 else ogate)[:, :, c:c + 512]
                act.activation(dst, ps[:, bank:bank + 2, :], ACT.Copy).then_inc(
                    s["inp_copied"] if b < 2 else s["og_copied"], 1)

            nh = nf + 8
            for lv in range(8):
                exp_level(lv)
                hi(nh + 3 + lv)
                if lv % 2 == 1:
                    copy_block(lv // 2)
            act.wait_ge(s["og_copied"], 2)
            for t in range(TT):
                ins = act.activation(ogate[:, t, :], ogate[:, t, :], ACT.Sigmoid)
            ins.then_inc(s["og_copied"], 1)
            act.wait_ge(s["cross_done"], 1)
            act.activation(pairs_x, ps[:, 4:6, :].rearrange("p a (b c) -> p (a b) c", c=P), ACT.Copy).then_inc(s["cross_copied"], 1)
            for t in range(TT):
                act.wait_ge(s["o_done"], t + 1)
                act.activation(xn[:, t, :].rearrange("p (a b) -> p a b", a=2), ps[:, 2 * t:2 * t + 2, :], ACT.Square,
                               accum_out=ssq[:, 8 + t:9 + t]).then_inc(s["ssq_ready"], 1)
            operand_hi(4, V_OUT)
            no = G["hout"]
            hi_of(no + 3, no + 4, no + 5)
            squares(5, s["h_added"], 4)
            hi(no + 6)
            operand_hi(5, V_FFN2)
            ffn(G["ffn1"], 1)
            squares(6, s["h_added"], 6)
            hi(G["mq"] + 2)
            act.wait_ge(s["bias_out"], 16)
            skew = bass.AP(bias_scratch.tensor, 0, [[1, P], [BIAS_LEN, HEADS], [1, S]])
            act.dma_start(bias, skew).then_inc(s["bias_in"], 16)
            operand_hi(6, V_MIX2 + 8)
            nm = G["mq"]

            def copy_qk(i):
                n = nm + (0, 1, 4, 5, 6, 7, 10, 11)[i]
                act.wait_ge(s["products_done"], n + 1)
                dst = (km_T if i % 2 else qm_T)[:, 2 * (i // 2):2 * (i // 2) + 2, :].rearrange("p a b -> p (a b)")
                act.activation(dst, ps[:, 6 + i % 2, :], ACT.Copy, scale=1.0 if i % 2 else MOBA_SCALE).then_inc(s["mqk_copied"], 1)

            def copy_v(b):
                act.wait_ge(s["products_done"], nm + (4, 10)[b])
                bank = (4, 6)[b]
                act.activation(v_m[:, :, 512 * b:512 * b + 512], ps[:, bank:bank + 2, :], ACT.Copy).then_inc(s["mv_copied"], 1)

            def scores2(u, j):
                n = P if (u - 16) % 2 == 0 else S
                return ps[:, 2 + u % 2, n * j:n * j + n], probm[:, u % 2, j, 0:n]

            def first_exps(u):
                act.wait_ge(s["neg_ready"], u + 1)
                for j in range(2):
                    src, dst = scores2(u, j)
                    ins = act.activation(dst, src, ACT.Exp, scale=1.0, bias=neg_max[:, j:j + 1], accum_out=row_sum[:, j:j + 1])
                ins.then_inc(s["exp_done"], 1)

            def copy_o2(u):
                t, j = (u - 16) % 2, (u - 16) // 2
                dst = (hid_hi if j < 2 else x_hi)[:, 2 * j:2 * j + 2, P * t:P * t + P]
                act.activation(dst,
                               ps[:, 4 + u % 2, 0:256].rearrange("p (a b) -> p a b", a=2), ACT.Copy).then_inc(s["mo_hi"], 1)

            copy_qk(0)
            hi(nm + 3)
            copy_qk(1)
            hi_of(nm + 4, nm + 5)
            first_exps(16)
            copy_v(0)
            hi(nm + 6)
            copy_qk(2)
            hi(nm + 7)
            copy_qk(3)
            hi(nm + 8)

            def fill_work2(u):
                for n in ahead2.get(u, ()):
                    hi(nm + n)
                if u in (16, 17):
                    copy_qk(u - 12)
                if u == 19:
                    copy_v(1)
                if u == 20:
                    copy_qk(6)
                    copy_qk(7)

            units(16, 8, lambda u: 1.0, scores2, copy_o2, fill_work2)
            no = G["mout"]
            hi_of(no + 4, no + 5)
            squares(7, s["h_added"], 8)
            hi(no + 6)
            operand_hi(7, V_FFN2 + 8)
            ffn(G["ffn2"], 2)
            squares(8, s["h_added"], 10)

        @block.vector
        def _(dve):
            then = Chain(dve, s["dve_step"])

            def lo(n, i=None):
                _, _, _, kc, _, cols = granules[n]
                sl = slice(0, kc * cols)
                dve.wait_ge(s["hi_ready"], (n + 1) if i is None else 6 * i + (n + 1))
                dve.tensor_tensor(w_lo[:, n % RING, sl], raw[:, n % RING, sl], f32(w_hi[:, n % RING, sl]), ALU.subtract).then_inc(s["lo_ready"], 1)

            def lo_of(*ns):
                for n in ns:
                    lo(n)

            def operand_lo(k, gain):
                for c in range(DC):
                    dve.wait_ge(s["xhi_ready"], DC * k + 2 * (c // 2) + 2)
                    dve.scalar_tensor_tensor(x_lo[:, c, :], ps[:, turn_bank(k) + c // 2, 256 * (c % 2):256 * (c % 2) + 256],
                                             1.0 if gain is None else vcol[:, 0, gain + c:gain + c + 1], f32(x_hi[:, c, :]),
                                             ALU.mult, ALU.subtract).then_inc(s["xlo_ready"], 1)

            def variance(m, t):
                c = 2 * m + t
                dve.wait_ge(s["ssq_ready"], c + 1)
                dve.tensor_scalar(var[:, c:c + 1], ssq[:, c:c + 1], 1.0 / D, EPS, ALU.mult, ALU.add).then_inc(s["var_ready"], 1)

            def normalize(m):
                for t in range(TT):
                    variance(m, t)
                for t in range(TT):
                    c = 2 * m + t
                    dve.wait_ge(s["rstd_ready"], c + 1)
                    dve.tensor_scalar(xn[:, t, :], h[:, t, :], rstd[:, c:c + 1], None, ALU.mult).then_inc(s["xn_ready"], 1)

            def add_down(n_last, f):
                for t in range(TT):
                    for c in range(2):
                        if t == 0 or c == 0:
                            dve.wait_ge(s["part_done"], 4 * f + 2 + 2 * t + c)
                        else:
                            dve.wait_ge(s["products_done"], n_last + 1)
                        hv = h[:, t, 512 * c:512 * c + 512]
                        ins = dve.tensor_tensor(hv, ps[:, 4 + 2 * c + t, :], hv, ALU.add)
                    ins.then_inc(s["h_added"], 1)

            def add_out(n0, k, bank0, bank1, half0=2):
                dve.wait_ge(s["products_done"], n0 + half0)
                dve.tensor_tensor(h[:, :, 0:512], ps[:, bank0:bank0 + 2, :], h[:, :, 0:512], ALU.add)
                lo(n0 + 5)
                for t in range(TT):
                    if t == 0:
                        dve.wait_ge(s["part_done"], 2 * k + 1)
                    else:
                        dve.wait_ge(s["products_done"], n0 + 4)
                    dve.tensor_tensor(h[:, t, 512:D], ps[:, bank1 + t, :], h[:, t, 512:D], ALU.add).then_inc(s["h_added"], 1)

            dve.memset(minus_half, -0.5).then_inc(s["setup"], 1)
            dve.memset(table[NBUCKET:NBUCKET + 1, :], -FAR).then_inc(s["setup"], 1)
            normalize(0)
            lo(0)
            operand_lo(0, V_MIX1)
            lo_of(1, 2)
            dve.wait_ge(s["pos_in"], 32)
            then(dve.tensor_copy(pos_col, pos_i[:, :]))
            dve.wait_ge(s["const_in"], 16)
            freq = const[:, K_FREQ:K_END]
            A0, A1, A2 = ang[:, 0, :], ang[:, 1, :], ang[:, 2, :]
            for t in range(TT):
                ins = dve.tensor_scalar(ang[:, 0, 24 * t:24 * t + 24], freq, pos_col[:, t:t + 1], None, ALU.mult)
            then(ins)
            turn = 2 * np.pi
            for unit in (4096.0, 1.0):
                full = turn * unit
                parts, rest = [], full
                for bits in (12, 12, 24):
                    e = int(np.floor(np.log2(abs(rest)))) - (bits - 1)
                    q = float(np.round(rest / 2.0 ** e) * 2.0 ** e)
                    parts.append(q)
                    rest -= q
                then(dve.tensor_scalar(A1, A0, float(np.float32(1 / full)), 12582912.0, ALU.mult, ALU.add))
                then(dve.tensor_scalar(A1, A1, 12582912.0, None, ALU.subtract))
                for q in parts:
                    then(dve.scalar_tensor_tensor(A0, A1, -q, A0, ALU.mult, ALU.add))
            then(dve.tensor_scalar(A0, A0, 3.1415925, -3.1415925, ALU.min, ALU.max))
            then(dve.tensor_scalar(A1, A0, -1.0, None, ALU.mult))
            then(dve.tensor_tensor(A1, A1, A0, ALU.min))
            dve.tensor_scalar(A1, A1, float(np.pi / 2), None, ALU.add).then_inc(s["setup"], 1)
            then(dve.tensor_copy(posrow, posrow_i))
            for t in range(TT):
                ins = dve.tensor_scalar(see[:, t, :], posrow, pos_col[:, t:t + 1], None, ALU.is_le)
            then(ins)
            then(dve.tensor_scalar(add_b, see, -1.0, FAR, ALU.add, ALU.mult))
            lo_of(*range(3, 10))
            dve.wait_ge(s["ssq6_ready"], 1)
            dve.tensor_scalar(var6[:, 0:2], ssq6[:, 0:2], 1.0 / HD, EPS, ALU.mult, ALU.add)
            dve.tensor_scalar(var6[:, 2:4], ssq6[:, 2:4], 1.0 / 256, EPS, ALU.mult, ALU.add)
            dve.tensor_scalar(var6[:, 4:6], ssq6[:, 4:6], 1.0 / P, EPS, ALU.mult, ALU.add).then_inc(s["var6_ready"], 1)
            dve.tensor_scalar(w_idx.rearrange("p (t h) -> p t h", t=TT), proj[:, :, C_IW:C_IW + HEADS], HEADS ** -0.5, None, ALU.mult)
            dve.wait_ge(s["rstd6_ready"], 1)
            dve.wait_ge(s["gain_in"], 16)
            for t in range(TT):
                ins = dve.scalar_tensor_tensor(proj[:, t, C_IK:C_IK + HD], proj[:, t, C_IK:C_IK + HD], rstd6[:, t:t + 1], g_ik,
                                               ALU.mult, ALU.mult)
            then(ins)
            dve.wait_ge(s["trig_ready"], 1)

            def rotate(x, heads, width, off, half, freq0, tmp):
                v = x.rearrange("p t (h w) -> p t h w", w=width)
                n = TT * heads * half
                t4 = [tmp[:, i, 0:n].rearrange("p (t h w) -> p t h w", t=TT, w=half) for i in range(4)]
                x1, x2 = v[:, :, :, off:off + half], v[:, :, :, off + half:off + 2 * half]
                cos = trig[:, 0, :, freq0:freq0 + half].unsqueeze(2).broadcast_to((P, TT, heads, half))
                sin = trig[:, 1, :, freq0:freq0 + half].unsqueeze(2).broadcast_to((P, TT, heads, half))
                dve.tensor_tensor(t4[0], x1, cos, ALU.mult)
                dve.tensor_tensor(t4[1], x2, sin, ALU.mult)
                dve.tensor_tensor(t4[2], x1, sin, ALU.mult)
                then(dve.tensor_tensor(t4[3], x2, cos, ALU.mult))
                dve.tensor_tensor(x1, t4[0], t4[1], ALU.subtract)
                return dve.tensor_tensor(x2, t4[2], t4[3], ALU.add)

            tmp_i = region(7632, 4, 160)
            rotate(proj[:, :, C_IQ:C_IW], 9, HD, 0, 8, 0, tmp_i).then_inc(s["idx_ready"], 1)
            lo_of(10, 11, 12)
            for c in range(3):
                dve.wait_ge(s["hhi_ready"], 2 if c < 2 else 3)
                ins = dve.scalar_tensor_tensor(hid_lo[:, c, :], ps[:, (5 + c // 2) % 2, 256 * (c % 2):256 * (c % 2) + 256],
                                               vcol[:, 0, V_CQ + c:V_CQ + c + 1], f32(hid_hi[:, c, :]), ALU.mult, ALU.subtract)
                ins.then_inc(s["hlo_ready"], 1)
            for n in range(8):
                t, j = n // 4, n % 4
                dve.wait_ge(s["relu_done"], n + 1)
                for hh in range(2):
                    w = w_idx[:, 8 * t + 2 * j + hh:8 * t + 2 * j + hh + 1]
                    if j == 0 and hh == 0:
                        ins = dve.tensor_scalar(isc[:, t, :], prob[:, n % 2, 0, :], w, None, ALU.mult)
                    else:
                        ins = dve.scalar_tensor_tensor(isc[:, t, :], prob[:, n % 2, hh, :], w, isc[:, t, :], ALU.mult, ALU.add)
                    if hh == 0:
                        then(ins)
                ins.then_inc(s["relu_used"], 1)
                dve.wait_ge(s["relu_used"], n + 1)
            then(dve.tensor_tensor(isc, isc, see, ALU.mult))
            then(dve.tensor_scalar(add_a, see, -1.0, MASKED, ALU.add, ALU.mult))
            then(dve.tensor_tensor(isc, isc, add_a, ALU.add))

            def largest():
                for t in range(TT):
                    ins = dve.max(top8[:, 8 * t:8 * t + 8], isc[:, t, :])
                then(ins)
                for t in range(TT):
                    ins = dve.match_replace(isc[:, t, :], top8[:, 8 * t:8 * t + 8], isc[:, t, :], TAKEN)
                then(ins)

            def choose_keys():
                then(dve.tensor_scalar(isc, isc, -2.0e38, None, ALU.is_le))
                then(dve.tensor_tensor(isc, isc, see, ALU.mult))
                then(dve.tensor_scalar(add_a, isc, -1.0, FAR, ALU.add, ALU.mult))

            dve.wait_ge(s["qb_copied"], 1)
            dve.wait_ge(s["kr_ready"], 1)
            rotate(proj[:, :, C_QB:C_QB + 768], HEADS, BQ, HD, 16, 8, pool_tmp).then_inc(s["qb_ready"], 1)
            g0 = G["gate"]
            lo(g0)

            def maxima(u):
                dve.wait_ge(s["scores_done"], u + 1)
                c = 2 * (u % 2)
                if u >= 2 and u not in (16, 17):
                    dve.wait_ge(s["probT_done"], u - 1)
                if u < 16:
                    m = (add_b if u < 8 else add_a)[:, u % 2, :].unsqueeze(1).broadcast_to((P, 2, S))
                    ins = dve.tensor_tensor(prob[:, u % 2], ps[:, 2 + u % 2, :].rearrange("p (a b) -> p a b", a=2), m, ALU.add)
                    ins.then_inc(s["scores_used"], 1)
                    dve.wait_ge(s["scores_used"], u + 1)
                    src, scale = prob[:, u % 2], (BQ ** -0.5 if u < 8 else HD ** -0.5)
                else:
                    n = P if (u - 16) % 2 == 0 else S
                    src, scale = ps[:, 2 + u % 2, 0:2 * n].rearrange("p (a b) -> p a b", a=2), 1.0
                then(dve.tensor_reduce(rowmax[:, c:c + 2], src, AX_X, ALU.max))
                dve.tensor_scalar(neg_max[:, c:c + 2], rowmax[:, c:c + 2], -scale, None, ALU.mult).then_inc(s["neg_ready"], 1)

            def units(first, count, extra):
                if first == 0:
                    maxima(first)
                for u in range(first, first + count):
                    c = 2 * (u % 2)
                    dve.wait_ge(s["exp_done"], u + 1)
                    then(dve.reciprocal(row_inv[:, c:c + 2], row_sum[:, c:c + 2]))
                    for j in range(2):
                        if u < 16:
                            p = prob[:, u % 2, j, :]
                        else:
                            p = probm[:, u % 2, j, 0:(P if (u - 16) % 2 == 0 else S)]
                        ins = dve.tensor_scalar(p, p, row_inv[:, c + j:c + j + 1], None, ALU.mult)
                    ins.then_inc(s["prob_ready"], 1)
                    if u < TOPK // 8:
                        largest()
                    if u == TOPK // 8 - 1:
                        choose_keys()
                    if u + 1 < first + count:
                        maxima(u + 1)
                    extra(u)

            def latent_lo(u):
                t, j = u % 2, (u % 8) // 2
                dve.wait_ge(s["o_copied"], u + 1)
                dve.tensor_tensor(hid_lo[:, j, P * t:P * t + P], ps[:, 4 + u % 2, 0:P], f32(hid_hi[:, j, P * t:P * t + P]),
                                  ALU.subtract).then_inc(s["ob_lo"], 1)

            def fill_lo(u):
                if 1 <= u <= 8:
                    latent_lo(u - 1)

            units(0, 16, fill_lo)
            for c in range(0, 4, 2):
                dve.wait_ge(s["ohi_ready"], c // 2 + 1)
                dve.tensor_tensor(x_lo[:, c:c + 2, :], o_T[:, c:c + 2, :], f32(x_hi[:, c:c + 2, :]), ALU.subtract).then_inc(s["olo_ready"], 1)
            ba = G["branch_a"]
            gate_b = gates[:, :, D:2 * D]
            dve.wait_ge(s["gate_sig"], 4)
            for c in range(2):
                sl = slice(512 * c, 512 * c + 512)
                dve.wait_ge(s["products_done"], ba + c + 1)
                if c == 0:
                    then(dve.tensor_tensor(xn[:, :, sl], ps[:, 0:2, :], gates[:, :, sl], ALU.mult))
                    dve.wait_ge(s["b_gated"], 1)
                    dve.tensor_tensor(xn[:, :, sl], xn[:, :, sl], gate_b[:, :, sl], ALU.add)
                else:
                    then(dve.tensor_tensor(xn[:, :, sl], ps[:, 2:4, :], gates[:, :, sl], ALU.mult))
                    for t in range(TT):
                        dve.tensor_tensor(xn[:, t, sl], xn[:, t, sl], gate_b[:, t, sl], ALU.add).then_inc(s["xn_ready"], 1)
            operand_lo(1, None)
            dve.wait_ge(s["lo_ready"], ba + 4)
            lo(ba + 4)
            lo_of(ba + 5)
            f0 = G["ffn0"]
            lo(f0)
            add_out(G["out"], 0, 4, 6)
            normalize(1)
            operand_lo(2, V_FFN1)
            lo_of(f0 + 2)

            def ffn(n0, f):
                def post(p, n_gate, i=None):
                    par = p % 2
                    P0 = PAIRS * f + p
                    more = 0 if i is None else 2 * i
                    done = 0 if i is None else 6 * i
                    if f == 0:
                        for ft in range(4):
                            col = 22 * (ft // 2) + 2 * p + ft % 2
                            first = 4 * p + ft + 1
                            both = 4 * p + 2 * (ft // 2) + 2
                            dve.wait_ge(s["conv_first"], both if i is None else 8 * i + both)
                            dst = conv[:, par, ft, :]
                            base = 256 * (ft % 2)
                            for tap in range(2):
                                back = 2 - tap
                                c = 44 * tap + col
                                w = vcol[:, 1, c:c + 1] if i is None else vcol[:, 1, bass.ds(i * 4 + c, 1)]
                                ins = dve.scalar_tensor_tensor(dst[:, back:S], ps[:, 2 * par + ft // 2, base:base + S - back], w,
                                                               dst[:, back:S], ALU.mult, ALU.add)
                                if tap == 0:
                                    ins.then_inc(s["conv_step"], 1)
                                    dve.wait_ge(s["conv_step"], first if i is None else 8 * i + first)
                        ins.then_inc(s["conv_done"], 1)
                        dve.wait_ge(s["gated"], more + P0 + 1)
                        dve.tensor_tensor(hid[:, par, :], act_g[:, par, :], conv[:, par, 2:4, :].rearrange("p a b -> p (a b)"),
                                          ALU.mult).then_inc(s["hid_ready"], 1)
                    else:
                        dve.wait_ge(s["products_done"], done + (n_gate + 2))
                        dve.wait_ge(s["gated"], more + P0 + 1)
                        dve.tensor_tensor(hid[:, par, :], act_g[:, par, :], ps[:, 2 * par + 1, :], ALU.mult).then_inc(s["hid_ready"], 1)

                def post_lo(p, i=None):
                    par = p % 2
                    first = 3 + PAIRS * f + p + 1
                    dve.wait_ge(s["hhi_ready"], first if i is None else 2 * i + first)
                    dve.tensor_tensor(hid_lo[:, 2 * par:2 * par + 2, :].rearrange("p a b -> p (a b)"), hid[:, par, :],
                                      f32(hid_hi[:, 2 * par:2 * par + 2, :].rearrange("p a b -> p (a b)")),
                                      ALU.subtract).then_inc(s["hlo_ready"], 1)

                lo(n0 + 3)
                post(0, n0)
                lo(n0 + 4)
                post_lo(0)
                lo(n0 + 5)
                post(1, n0 + 2)
                lo(n0 + 6)
                post_lo(1)
                lo(n0 + 7)
                with dve.Fori(0, 4) as i:
                    for q in range(2):
                        lo(n0 + 8 + 3 * q, i)
                        post(2 + q, n0 + 5 + 3 * q, i)
                        lo(n0 + 9 + 3 * q, i)
                        post_lo(2 + q, i)
                        lo(n0 + 10 + 3 * q, i)
                n1 = n0 + 29
                lo_next(n1 + 3)
                post(10, n1)
                lo_next(n1 + 4)
                post_lo(10)
                lo_next(n1 + 5)
                add_down(n1 + 3, f)

            def lo_next(n):
                if n < G["end"]:
                    lo(n)

            ffn(f0, 0)

            def final_norm(m, gain_in):
                for t in range(TT):
                    variance(m, t)
                dve.wait_ge(s[gain_in], 16)
                for t in range(TT):
                    c = 2 * m + t
                    dve.wait_ge(s["rstd_ready"], c + 1)
                    dve.scalar_tensor_tensor(h[:, t, :], h[:, t, :], rstd[:, c:c + 1], g_final[:, :],
                                             ALU.mult, ALU.mult).then_inc(s["h_final"], 1)

            final_norm(2, "final_in")
            normalize(3)
            operand_lo(3, V_MIX2)
            lo(G["hf"] + 2)
            lbl = [vcol[:, 0, V_LB + 8 * r:V_LB + 8 * r + 8] for r in range(2)]
            then(dve.tensor_tensor(lb, lbl[0], lbl[1], ALU.max))
            dve.tensor_tensor(lb_tmp[:, 0:8], lbl[0], lb, ALU.subtract)
            dve.tensor_tensor(lb_tmp[:, 8:16], lbl[1], lb, ALU.subtract).then_inc(s["lb_ready"], 1)
            dve.wait_ge(s["lb_ready"], 2)
            then(dve.tensor_tensor(lb_rest, lb_tmp[:, 0:8], lb_tmp[:, 8:16], ALU.add))
            then(dve.reciprocal(lb_rest, lb_rest))
            then(dve.tensor_tensor(lb, lb_tmp[:, 0:8], lb_rest, ALU.mult))
            then(dve.tensor_scalar(lb_rest, lb, -1.0, 1.0, ALU.mult, ALU.add))
            dve.memset(ones, 1.0)
            dve.memset(pairs.rearrange("p a b c -> p (a b c)"), 0.0)
            nf = G["hf"]
            F = E[:, 0]
            for j in range(4):
                dve.wait_ge(s["f_sig"], j + 1)
                for hh in (2 * j, 2 * j + 1):
                    ins = dve.tensor_scalar(F[:, hh, :], K[:, hh, :], lb_rest[:, hh:hh + 1], lb[:, hh:hh + 1], ALU.mult, ALU.add)
                then(ins)
                lo(nf + 3 + j)
            dve.tensor_scalar(K.rearrange("p a b -> p (a b)"), F.rearrange("p a b -> p (a b)"), -1.0, 1.0, ALU.mult, ALU.add).then_inc(s["f_ready"], 1)
            for j in range(4):
                lo(nf + 7 + j)
            dve.wait_ge(s["logf_done"], 1)
            for hh in range(HEADS):
                for t in range(TT):
                    seg = CUM[:, hh, P * t:P * t + P]
                    ins = dve.tensor_tensor_scan(seg, ones, seg, 0.0, ALU.mult, ALU.add)
            ins.then_inc(s["cum_ready"], 1)
            dve.wait_ge(s["masks_in"], 16)

            def choose(level, count):
                for j in range(4):
                    dve.wait_ge(s["pairs_done"], 4 * count + j + 1)
                    dst = pairs[:, j // 2, 4 * (j % 2):4 * (j % 2) + 4, :]
                    m = masks[:, level, :].unsqueeze(1).broadcast_to((P, 4, P))
                    dve.copy_predicated(dst, m, ps[:, j, :].rearrange("p (a b) -> p a b", a=4)).then_inc(s["pairs_used"], 1)

            def decayed(lv):
                b = LEVELS[lv] if lv < len(LEVELS) else P
                dve.wait_ge(s["e_exp"], lv + 1)
                flat = lambda v: v.rearrange("p h t -> p (h t)").rearrange("p (g w) -> p g w", w=2 * b)
                e, q, k = flat(E[:, lv % 2]), flat(Q), flat(K)
                dve.tensor_tensor(e[:, :, b:2 * b], e[:, :, b:2 * b], q[:, :, b:2 * b], ALU.mult).then_inc(s["x_ready"], 1)
                dve.tensor_tensor(e[:, :, 0:b], e[:, :, 0:b], k[:, :, 0:b], ALU.mult).then_inc(s["x_ready"], 1)

            dve.wait_ge(s["q_ready"], 4)
            choose(len(LEVELS), 0)
            nh = nf + 8
            for lv in range(len(LEVELS)):
                decayed(lv)
                lo(nh + 3 + lv)
                if lv == len(LEVELS) - 1:
                    decayed(len(LEVELS))
                choose(lv, lv + 1)
            lo(nh + 10)
            for t in range(TT):
                variance(4, t)
            dve.wait_ge(s["og_copied"], 3)
            for t in range(TT):
                dve.wait_ge(s["rstd_ready"], 8 + t + 1)
                dve.scalar_tensor_tensor(xn[:, t, :].rearrange("p (a b) -> p a b", a=2), ps[:, 2 * t:2 * t + 2, :],
                                         rstd[:, 8 + t:9 + t], ogate[:, t, :].rearrange("p (a b) -> p a b", a=2),
                                         ALU.mult, ALU.mult).then_inc(s["xn_ready"], 1)
            operand_lo(4, V_OUT)
            no = G["hout"]
            lo_of(no + 3, no + 4)
            add_out(no, 2, 0, 2)
            normalize(5)
            operand_lo(5, V_FFN2)
            lo(no + 6)
            ffn(G["ffn1"], 1)
            normalize(6)
            operand_lo(6, V_MIX2 + 8)
            nm = G["mq"]
            lo_of(nm + 2, nm + 3, nm + 4, nm + 5)
            maxima(16)
            lo_of(nm + 6, nm + 7, nm + 8)

            def output_lo(u):
                t, j = (u - 16) % 2, (u - 16) // 2
                dve.wait_ge(s["mo_hi"], u - 15)
                dst = slice(P * t, P * t + P)
                hi_part, lo_part = (hid_hi, hid_lo) if j < 2 else (x_hi, x_lo)
                dve.tensor_tensor(lo_part[:, 2 * j:2 * j + 2, dst], ps[:, 4 + u % 2, 0:256].rearrange("p (a b) -> p a b", a=2),
                                  f32(hi_part[:, 2 * j:2 * j + 2, dst]), ALU.subtract).then_inc(s["mo_lo"], 1)

            def fill_lo2(u):
                if u > 16:
                    output_lo(u - 1)

            units(16, 8, fill_lo2)
            output_lo(23)
            no = G["mout"]
            dve.wait_ge(s["lo_ready"], no + 4)
            lo(no + 4)
            add_out(no, 4, 6, 2, half0=3)
            normalize(7)
            operand_lo(7, V_FFN2 + 8)
            lo(no + 6)
            ffn(G["ffn2"], 2)
            final_norm(8, "final2_in")

        @block.tensor
        def _(pe):
            parts = ((x_hi, w_hi), (x_hi, w_lo), (x_lo, w_hi))
            hid_parts = ((hid_hi, w_hi), (hid_hi, w_lo), (hid_lo, w_hi))

            def split_ready(n, i=None):
                pe.wait_ge(s["lo_ready"], (n + 1) if i is None else 6 * i + (n + 1))

            def token_product(n, chunks, bank, first, last, ops=parts, i=None, ready=None, part=None, by_tile=False):
                if part != 1:
                    split_ready(n, i)
                _, _, _, kc, _, cols = granules[n]
                wide = (cols + 511) // 512
                ks = {None: range(kc), 0: range(kc // 2), 1: range(kc // 2, kc)}[part]
                if by_tile:
                    order = [(kk, t, c) for t in range(TT) for c in range(wide) for kk in ks]
                else:
                    order = [(kk, t, c) for kk in ks for t in range(TT) for c in range(wide)]
                for kk, t, c in order:
                    if ready and t == 0:
                        ready(chunks + kk)
                    w0 = kk * cols + 512 * c
                    n_c = min(512, cols - 512 * c)
                    for q, (x, w) in enumerate(ops):
                        ins = pe.matmul(ps[:, bank + 2 * c + t, 0:n_c], x[:, chunks + kk, P * t:P * t + P],
                                        w[:, n % RING, w0:w0 + n_c],
                                        start=(first and kk == 0 and q == 0), stop=(last and kk == kc - 1 and q == 2))
                    if by_tile and kk == kc - 1 and (t, c) != (TT - 1, wide - 1):
                        ins.then_inc(s["part_done"], 1)
                if part != 0:
                    ins.then_inc(s["products_done"], 1)

            def feature_product(n, bank, i=None, ready=None):
                split_ready(n, i)
                for f in range(2):
                    for k in range(DC):
                        if ready and f == 0:
                            ready(k)
                        for q, (x, w) in enumerate(parts):
                            ins = pe.matmul(ps[:, bank, S * f:S * f + S], w[:, n % RING, 256 * k + P * f:256 * k + P * f + P],
                                            x[:, k, :], start=(k == 0 and q == 0), stop=(k == DC - 1 and q == 2))
                ins.then_inc(s["products_done"], 1)

            def turn_xn(k):
                for t in range(TT):
                    pe.wait_ge(s["xn_ready"], 2 * k + t + 1)
                    for c in range(DC):
                        ins = pe.transpose(ps[:, turn_bank(k) + c // 2, 256 * (c % 2) + P * t:256 * (c % 2) + P * t + P],
                                           xn[:, t, P * c:P * c + P], ident)
                        if t == 1 and c % 2 == 1:
                            ins.then_inc(s["xt_done"], 1)

            def operand_ready(k):
                return lambda c: pe.wait_ge(s["xlo_ready"], DC * k + c + 1)

            pe.wait_ge(s["const_in"], 16)
            turn_xn(0)
            pe.wait_ge(s["small_in"], 16 * 12)
            for g, n in ((0, 75), (1, 88), (2, 88)):
                ins = pe.transpose(ps[:, 4, 88 * g:88 * g + n], vrow[0:n, g, :], ident[0:n, 0:n])
            ins.then_inc(s["vrow_T"], 1)
            pe.wait_ge(s["table_in"], 16)
            pe.wait_ge(s["setup"], 2)
            pe.matmul(ps[0:HEADS, 5, 0:BIAS_LEN], table[:, :], const[0:NBUCKET + 1, K_BUCKET:K_BUCKET + BIAS_LEN],
                      start=True, stop=True).then_inc(s["bias_ps"], 1)
            pe.wait_ge(s["bias_sb"], 1)
            for b in range(4):
                if b >= 2:
                    pe.wait_ge(s["proj_copied"], b - 1)
                bank = 4 + 2 * (b % 2)
                token_product(2 * b, 0, bank, True, False, ready=operand_ready(0) if b == 0 else None)
                token_product(2 * b + 1, 4, bank, False, True, ready=operand_ready(0) if b == 0 else None)

            pe.wait_ge(s["proj_copied"], 3)
            token_product(G["gate0"], 0, 4, True, False)
            token_product(G["gate0"] + 1, 4, 4, False, True)
            groups = [0]

            def turn_group(pieces):
                n = groups[0]
                if n >= 2 and n != 7 and n != 8:
                    pe.wait_ge(s["group_copied"], n - 1 if n < 7 else n - 3)
                if n in (7, 8):
                    pe.wait_ge(s["hlo_ready"], 2 if n == 7 else 3)
                for i, piece in enumerate(pieces):
                    ins = pe.transpose(ps[0:piece.shape[1], n % 2, P * i:P * i + P], piece, ident)
                ins.then_inc(s["group_done"], 1)
                groups[0] += 1

            pe.wait_ge(s["idx_ready"], 1)
            turn_group([proj[:, t, C_IK:C_IK + HD] for t in range(TT)])
            for j in range(4):
                turn_group([proj[:, t, C_IQ + HD * hh:C_IQ + HD * hh + HD] for hh in (2 * j, 2 * j + 1) for t in range(TT)])
            pe.wait_ge(s["c_scaled"], 1)
            turn_group([proj[:, t, C_CQ + P * c:C_CQ + P * c + P] for c in range(2) for t in range(TT)])
            turn_group([proj[:, t, C_CKV:C_CKV + P] for t in range(TT)])
            pe.wait_ge(s["kr_ready"], 1)
            pe.wait_ge(s["qk_ready"], 1)
            turn_group([proj[:, t, C_G - BQ:C_G] for t in range(TT)])
            turn_group([proj[:, t, C_AK + HD * g:C_AK + HD * g + HD] for g in range(KV_HEADS) for t in range(TT)])
            for j in range(4):
                turn_group([proj[:, t, HD * hh:HD * hh + HD] for hh in (2 * j, 2 * j + 1) for t in range(TT)])
            for n in range(8):
                t, j = n // 4, n % 4
                if n >= 2:
                    pe.wait_ge(s["relu_done"], n - 1)
                for hh in range(2):
                    ins = pe.matmul(ps[:, 2 + n % 2, S * hh:S * hh + S], qi_T[:, 2 * j + hh, P * t:P * t + P], ki_T, start=True, stop=True)
                ins.then_inc(s["dots_done"], 1)
            n = G["uq"]
            split_ready(n)
            pe.wait_ge(s["proj_copied"], 4)
            pe.wait_ge(s["gate_copied"], 1)
            for t in range(TT):
                for half in range(2):
                    for k in range(2):
                        for q, (x, w) in enumerate(hid_parts):
                            ins = pe.matmul(ps[:, 4 + 2 * t + half, 0:384], x[:, k, P * t:P * t + P],
                                            w[:, n % RING, 768 * k + 384 * half:768 * k + 384 * half + 384],
                                            start=(k == 0 and q == 0), stop=(k == 1 and q == 2))
            ins.then_inc(s["products_done"], 1)
            n = G["uk"]
            split_ready(n)
            pe.wait_ge(s["group_copied"], 11)
            for j in range(4):
                for q, (x, w) in enumerate(hid_parts):
                    ins = pe.matmul(ps[:, j // 2, S * (j % 2):S * (j % 2) + S], w[:, n % RING, P * j:P * j + P], x[:, 2, :],
                                    start=(q == 0), stop=(q == 2))
            ins.then_inc(s["products_done"], 1)
            n = G["uv"]
            split_ready(n)
            pe.wait_ge(s["relu_done"], 8)
            for t in range(TT):
                for q, (x, w) in enumerate(hid_parts):
                    ins = pe.matmul(ps[:, 2 + t, :], x[:, 2, P * t:P * t + P], w[:, n % RING, 0:512], start=(q == 0), stop=(q == 2))
            ins.then_inc(s["products_done"], 1)
            pe.wait_ge(s["qb_ready"], 1)
            pe.wait_ge(s["kv_copied"], 1)
            for j in range(4):
                turn_group([proj[:, t, C_QB + BQ * hh:C_QB + BQ * hh + BQ] for hh in (2 * j, 2 * j + 1) for t in range(TT)])
            pe.wait_ge(s["group_copied"], 15)

            def units(first, count, scores, values, sizes, extra):
                def score(u):
                    if u >= first + 2:
                        if u < 16:
                            pe.wait_ge(s["scores_used"], u - 1)
                        else:
                            pe.wait_ge(s["exp_done"], u - 1)
                    scores(u).then_inc(s["scores_done"], 1)

                def value(u):
                    pe.wait_ge(s["probT_copied"], u + 1)
                    if u >= first + 2:
                        if u < 10:
                            pe.wait_ge(s["ob_lo"], u - 1)
                        elif u < 16:
                            pe.wait_ge(s["o_copied"], u - 1)
                        else:
                            pe.wait_ge(s["mo_lo"], u - 17)
                    values(u).then_inc(s["pv_done"], 1)

                if first == 0:
                    score(first)
                for u in range(first, first + count):
                    if u + 1 < first + count:
                        score(u + 1)
                    if u > first:
                        value(u - 1)
                    pe.wait_ge(s["prob_ready"], u + 1)
                    if u >= first + 2:
                        pe.wait_ge(s["probT_copied"], u - 1)
                    buf, kt = sizes(u)
                    for j in range(2):
                        for k in range(kt):
                            ins = pe.transpose(ps[:, u % 2, P * (kt * j + k):P * (kt * j + k) + P], buf[:, u % 2, j, P * k:P * k + P], ident)
                    ins.then_inc(s["probT_done"], 1)
                    extra(u)
                value(first + count - 1)

            def scores1(u):
                t, j = u % 2, (u % 8) // 2
                for hh in range(2):
                    head = 2 * j + hh
                    q, k = (qb_T, kb_T[:, head, :]) if u < 8 else (qa_T, ka_T[:, head // 4, :])
                    ins = pe.matmul(ps[:, 2 + u % 2, S * hh:S * hh + S], q[:, head, P * t:P * t + P], k, start=True, stop=True)
                return ins

            def values1(u):
                j = (u % 8) // 2
                for hh in range(2):
                    head = 2 * j + hh
                    for k in range(TT):
                        v = v_b[:, k, HD * head:HD * head + HD] if u < 8 else proj[:, k, C_AV + HD * (head // 4):C_AV + HD * (head // 4) + HD]
                        ins = pe.matmul(ps[HD * hh:HD * hh + HD, 4 + u % 2, 0:P], v, prob_T[:, u % 2, hh, k, :], start=(k == 0), stop=(k == TT - 1))
                return ins

            g0 = G["gate"]

            bb, ba = G["branch_b"], G["branch_a"]

            def filler(u):
                r, half = u // 2, u % 2
                if r < 6:
                    if half == 0 and r % 2 == 0 and r >= 2:
                        pe.wait_ge(s["gate_copied"], 1 + r // 2)
                    token_product(g0 + r, 4 * (r % 2), 6, r % 2 == 0, r % 2 == 1, part=half)
                else:
                    if half == 0:
                        pe.wait_ge(s["gate_copied"] if r == 6 else s["yb_copied"], 4 if r == 6 else 1)
                        pe.wait_ge(s["ob_lo"], 8)
                    token_product(bb + r - 6, 0, 6, True, True, hid_parts, part=half)

            units(0, 16, scores1, values1, lambda u: (prob, TT), filler)
            pe.wait_ge(s["o_copied"], 16)
            for c in range(2):
                token_product(ba + c, 0, 2 * c, True, True,
                              ready=(lambda k: pe.wait_ge(s["olo_ready"], k // 2 + 1)) if c == 0 else None)
            turn_xn(1)

            def out_product(n0, bank0, bank1, ready, done=0):
                for g in range(done, 4):
                    c, k = g // 2, g % 2
                    token_product(n0 + g, 4 * k, (bank0, bank1)[c], k == 0, k == 1, ready=ready if c == 0 else None, by_tile=(g == 3))

            out_product(G["out"], 4, 6, operand_ready(1))
            turn_xn(2)

            def ffn(n0, f, k_turn):
                def up(p, n, i=None, ready=None):
                    par = p % 2
                    P0 = PAIRS * f + p
                    more = 0 if i is None else 2 * i
                    if p >= 2:
                        pe.wait_ge(s["conv_done"] if f == 0 else s["hid_ready"], more + P0 - 1)
                    feature_product(n, 2 * par, i, ready)
                    feature_product(n + 1, 2 * par + 1, i)

                def down(p, n, i=None, last=False):
                    first = 3 + PAIRS * f + p + 1
                    pe.wait_ge(s["hlo_ready"], first if i is None else 2 * i + first)
                    token_product(n, 2 * (p % 2), 4, p == 0, last, hid_parts, i=i, by_tile=last)

                up(0, n0, ready=operand_ready(k_turn))
                up(1, n0 + 2)
                down(0, n0 + 4)
                with pe.Fori(0, 4) as i:
                    for q in range(2):
                        up(2 + q, n0 + 5 + 3 * q, i)
                        down(1 + q, n0 + 7 + 3 * q, i)
                up(10, n0 + 29)
                down(9, n0 + 31)
                down(10, n0 + 32, last=True)

            ffn(G["ffn0"], 0, 2)
            turn_xn(3)
            nf = G["hf"]
            for j in range(8):
                feature_product(nf + j, j, ready=operand_ready(3) if j == 0 else None)

            def products(level, count):
                for j in range(4):
                    t = j // 2
                    if count == 0:
                        pe.wait_ge(s["f_sig"], 4)
                    else:
                        pe.wait_ge(s["pairs_used"], 4 * (count - 1) + j + 1)
                    for hh in range(4):
                        head = 4 * (j % 2) + hh
                        tok = slice(P * t, P * t + P)
                        k, q = (K, Q) if count == 0 else (E[:, (count - 1) % 2], E[:, (count - 1) % 2])
                        ins = pe.matmul(ps[:, j, P * hh:P * hh + P], k[:, head, tok], q[:, head, tok], start=True, stop=True)
                    ins.then_inc(s["pairs_done"], 1)

            pe.wait_ge(s["q_ready"], 4)
            pe.wait_ge(s["f_ready"], 1)
            nh = nf + 8
            for n in range(8):
                block_n, bank = n // 2, 4 + 2 * (n // 2 % 2)
                if n in (4, 6):
                    pe.wait_ge(s["inp_copied"], block_n - 1)
                token_product(nh + n, 4 * (n % 2), bank, n % 2 == 0, n % 2 == 1)
                if n >= 1:
                    pe.wait_ge(s["x_ready"], 2 * n)
                products(n - 1, n)
            pe.wait_ge(s["x_ready"], 2 * (len(LEVELS) + 1))
            pe.wait_ge(s["og_copied"], 2)
            last_e = E[:, len(LEVELS) % 2]
            for head in range(HEADS):
                ins = pe.matmul(ps[:, 4 + head // 4, P * (head % 4):P * (head % 4) + P], last_e[:, head, 0:P], last_e[:, head, P:S], start=True, stop=True)
            ins.then_inc(s["cross_done"], 1)
            pe.wait_ge(s["pairs_used"], 32)
            pe.wait_ge(s["inp_copied"], 2)
            pe.wait_ge(s["cross_copied"], 1)
            for t in range(TT):
                for head in range(HEADS):
                    dst = ps[:, 2 * t + head // 4, P * (head % 4):P * (head % 4) + P]
                    cols = slice(P * head, P * head + P)
                    ins = pe.matmul(dst, pairs[:, t, head, :], inp[:, t, cols], start=True, stop=(t == 0))
                    if t == 1:
                        ins = pe.matmul(dst, pairs_x[:, head, :], inp[:, 0, cols], start=False, stop=True)
                ins.then_inc(s["o_done"], 1)
            turn_xn(4)
            out_product(G["hout"], 0, 2, operand_ready(4))
            turn_xn(5)
            ffn(G["ffn1"], 1, 5)
            turn_xn(6)
            nm = G["mq"]

            def qk_product(i):
                if i >= 2:
                    pe.wait_ge(s["mqk_copied"], i - 1)
                if i >= 6:
                    pe.wait_ge(s["mv_copied"], 2)
                feature_product(nm + (0, 1, 4, 5, 6, 7, 10, 11)[i], 6 + i % 2, ready=operand_ready(6) if i == 0 else None)

            qk_product(0)
            qk_product(1)
            token_product(nm + 2, 0, 4, True, False)
            pe.wait_ge(s["bias_in"], 16)

            def scores2(u):
                t, j = (u - 16) % 2, (u - 16) // 2
                n = P if t == 0 else S
                pe.wait_ge(s["mqk_copied"], 2 * j + 2)
                for hh in range(2):
                    head = 2 * j + hh
                    dst = ps[:, 2 + u % 2, n * hh:n * hh + n]
                    pe.matmul(dst, qm_T[:, head, P * t:P * t + P], km_T[:, head, 0:n], start=True, stop=False)
                    ins = pe.matmul(dst, reverse, bias[:, head, S - n:S], start=False, stop=True)
                return ins

            def values2(u):
                t, j = (u - 16) % 2, (u - 16) // 2
                kt = 1 + t
                pe.wait_ge(s["mv_copied"], 1 + j // 2)
                flat = probm_T[:, u % 2].rearrange("p a b c -> p (a b c)")
                for hh in range(2):
                    head = 2 * j + hh
                    for k in range(kt):
                        at = P * (kt * hh + k)
                        ins = pe.matmul(ps[:, 4 + u % 2, P * hh:P * hh + P], v_m[:, k, P * head:P * head + P],
                                        flat[:, at:at + P], start=(k == 0), stop=(k == kt - 1))
                return ins

            def filler2(u):
                if u == 16:
                    qk_product(4)
                if u == 17:
                    qk_product(5)
                if u in (18, 19):
                    if u == 18:
                        pe.wait_ge(s["mqk_copied"], 6)
                    token_product(nm + 8 + u - 18, 4 * (u - 18), 6, u == 18, u == 19)
                if u == 20:
                    qk_product(6)
                    qk_product(7)
                if u in (21, 22):
                    if u == 21:
                        pe.wait_ge(s["mqk_copied"], 8)
                        pe.wait_ge(s["mo_lo"], 4)
                    token_product(G["mout"], 0, 6, True, False, hid_parts, part=u - 21)
                if u == 23:
                    pe.wait_ge(s["exp_done"], 24)
                    token_product(G["mout"] + 1, 0, 2, True, False, hid_parts)

            scores2(16).then_inc(s["scores_done"], 1)
            token_product(nm + 3, 4, 4, False, True)
            qk_product(2)
            qk_product(3)
            units(16, 8, scores2, values2, lambda u: (probm, 1 + (u - 16) % 2), filler2)
            pe.wait_ge(s["mo_lo"], 8)
            for c in range(2):
                token_product(G["mout"] + 2 + c, 4, (6, 2)[c], False, True, by_tile=(c == 1))
            turn_xn(7)
            ffn(G["ffn2"], 2, 7)


_INS = ["x", "positions", "norm_mix_g", "w_in", "idx_k_norm_g", "q_a_norm_g", "kv_a_norm_g", "w_uq", "w_uk", "w_uv",
        "w_branch_a", "w_branch_b", "w_out", "norm_ffn_g", "w_up", "conv_w", "conv_b", "w_down", "norm_final_g",
        "norm_mix_2", "norm_ffn_2", "hgrn_w_in_2", "hgrn_lb_logits_2", "hgrn_out_norm_2", "hgrn_w_out_2",
        "moba_w_in_2", "moba_w_out_2", "rel_bias_table_2", "ffn_w13_2", "ffn_w2_2", "final_norm_2"]


def kernel(**inputs):
    import concourse.bacc as _bacc
    from concourse import mybir as _mybir
    from concourse.bass_utils import run_bass_kernel_spmd as _run

    nc = _bacc.Bacc("TRN2", target_bir_lowering=False, num_devices=1)
    arrays, args = {}, {}
    const, pair_masks = shape_constants()
    given = {name: inputs[name] for name in _INS}
    given["const"], given["pair_masks"] = const, pair_masks
    for name, value in given.items():
        v = np.ascontiguousarray(value)
        arrays[f"in_{name}"] = v
        args[name] = nc.dram_tensor(f"in_{name}", v.shape, _mybir.dt.from_np(v.dtype), kind="ExternalInput").ap()
    out = nc.dram_tensor("out", (1, S, D), _mybir.dt.float32, kind="ExternalOutput").ap()
    build(nc, args, out)
    return _run(nc, [arrays], core_ids=[0]).results[0]["out"]
```
